# Optimizing a Trainium2 kernel written in Bass

```python
import jax, jax.numpy as jnp
from jax import lax
import numpy as np

D_MODEL = 1024
BATCH = 1
SEQ = 256
DEPTH = 2
DEC_BATCH = 8
DEC_SEQ = 8
PAST_LEN = 2048
PAGE_SIZE = 128

A_HEADS = 8
A_HEAD_DIM = 64
A_WIDTH = A_HEADS * A_HEAD_DIM
DECAY_LORA = 64
AAA_LORA = 64
GATE_LORA = 128
A_PROJ = 3 * A_WIDTH + DECAY_LORA + AAA_LORA + GATE_LORA
B_BLOCKS = 8
B_WIDTH = 512
B_BLOCK = B_WIDTH // B_BLOCKS
CONV_W = 4
LRU_C = 8.0
C_HEADS = 4
C_KDIM = 128
C_VDIM = 128
C_KWIDTH = C_HEADS * C_KDIM
C_WIDTH = C_HEADS * C_VDIM
CHUNK = 64
N_IN = A_PROJ + 2 * B_WIDTH + 2 * C_KWIDTH + 2 * C_WIDTH + 3 * D_MODEL
D_FF = 2816
RMS_EPS = 1e-6
GN_EPS = 64e-5

kernel_name = 'hybrid_rwkv7_rglru_hgrn2_decode_step'

def rmsnorm(x, g):
    xf = x.astype(jnp.float32)
    y = xf * lax.rsqrt(jnp.mean(xf * xf, axis=-1, keepdims=True) + RMS_EPS)
    return (y * g.astype(jnp.float32)).astype(x.dtype)

def swiglu(x, wg, wu, wd):
    return (jax.nn.silu(x @ wg) * (x @ wu)) @ wd

def rwkv7_mixer(p, shift_prev, s0, mu, w0, w2, a0, a2, g2, k_k, k_a, r_k, ln_g, ln_b):
    f32 = jnp.float32
    bsz, t_len, _ = p.shape
    prev = jnp.concatenate([shift_prev[:, None, :].astype(p.dtype), p[:, :-1]], axis=1)
    xs = p + mu * (prev - p)
    r, k, v, w1, a1, g1 = jnp.split(xs, [A_WIDTH, 2 * A_WIDTH, 3 * A_WIDTH, 3 * A_WIDTH + DECAY_LORA, 3 * A_WIDTH + DECAY_LORA + AAA_LORA], axis=-1)
    w = -jax.nn.softplus(-(w0 + jnp.tanh(w1) @ w2).astype(f32)) - 0.5
    decay = jnp.exp(-jnp.exp(w))
    a = jax.nn.sigmoid((a0 + a1 @ a2).astype(f32))
    g = (jax.nn.sigmoid(g1) @ g2).astype(f32)
    hs = (bsz, t_len, A_HEADS, A_HEAD_DIM)
    hp = (A_HEADS, A_HEAD_DIM)
    r = r.astype(f32).reshape(hs)
    k = k.astype(f32).reshape(hs)
    v = v.astype(f32).reshape(hs)
    decay = decay.reshape(hs)
    a = a.reshape(hs)
    kk = k * k_k.astype(f32).reshape(hp)
    kk = kk / jnp.maximum(jnp.sqrt(jnp.sum(kk * kk, axis=-1, keepdims=True)), 1e-12)
    k = k * (1.0 + (a - 1.0) * k_a.astype(f32).reshape(hp))

    def step(s, inp):
        r_t, w_t, k_t, v_t, kk_t, b_t = inp
        s_kk = jnp.einsum('bhvk,bhk->bhv', s, -kk_t)
        s = s * w_t[:, :, None, :] + s_kk[..., None] * b_t[:, :, None, :] + v_t[..., None] * k_t[:, :, None, :]
        return s, jnp.einsum('bhvk,bhk->bhv', s, r_t)

    xs_t = tuple(jnp.moveaxis(z, 1, 0) for z in (r, decay, k, v, kk, kk * a))
    s_last, y = lax.scan(step, s0.astype(f32), xs_t)
    y = jnp.moveaxis(y, 0, 1)
    mean = jnp.mean(y, axis=-1, keepdims=True)
    var = jnp.mean(jnp.square(y - mean), axis=-1, keepdims=True)
    y = (y - mean) * lax.rsqrt(var + GN_EPS) * ln_g.astype(f32).reshape(hp) + ln_b.astype(f32).reshape(hp)
    y = y + jnp.sum(r * k * r_k.astype(f32), axis=-1, keepdims=True) * v
    out = (y.reshape(bsz, t_len, A_WIDTH) * g).astype(p.dtype)
    return out, p[:, -1], s_last

def _lin_combine(earlier, later):
    a1, b1 = earlier
    a2, b2 = later
    return a1 * a2, a2 * b1 + b2

def rglru_mixer(p, conv_prev, h0, conv_w, conv_b, wa, ba, wx, bx, lam):
    f32 = jnp.float32
    bsz, t_len, _ = p.shape
    xb, gb = jnp.split(p, [B_WIDTH], axis=-1)
    xpad = jnp.concatenate([conv_prev.astype(p.dtype), xb], axis=1)
    xc = conv_b
    for j in range(CONV_W):
        xc = xc + xpad[:, j:j + t_len] * conv_w[j]
    xh = xc.reshape(bsz, t_len, B_BLOCKS, B_BLOCK)
    r = jax.nn.sigmoid((jnp.einsum('btgi,gij->btgj', xh, wa).reshape(bsz, t_len, B_WIDTH) + ba).astype(f32))
    i = jax.nn.sigmoid((jnp.einsum('btgi,gij->btgj', xh, wx).reshape(bsz, t_len, B_WIDTH) + bx).astype(f32))
    log_a = -LRU_C * r * jax.nn.softplus(-lam.astype(f32))
    a = jnp.exp(log_a)
    b = jnp.sqrt(-jnp.expm1(2.0 * log_a)) * i * xc.astype(f32)
    a_cum, b_cum = lax.associative_scan(_lin_combine, (a, b), axis=1)
    h = a_cum * h0.astype(f32)[:, None, :] + b_cum
    out = (h * jax.nn.gelu(gb.astype(f32))).astype(p.dtype)
    return out, xpad[:, t_len:], h[:, -1]

def hgrn2_mixer(p, s0, lb, norm_g):
    f32 = jnp.float32
    bsz, t_len, _ = p.shape
    q, fz, iv, gz = jnp.split(p, [C_KWIDTH, 2 * C_KWIDTH, 2 * C_KWIDTH + C_WIDTH], axis=-1)
    q = jax.nn.silu(q.astype(f32)).reshape(bsz, t_len, C_HEADS, C_KDIM)
    f = lb + (1.0 - lb) * jax.nn.sigmoid(fz.astype(f32))
    logf = jnp.log(f).reshape(bsz, t_len, C_HEADS, C_KDIM)
    k = (1.0 - f).reshape(bsz, t_len, C_HEADS, C_KDIM)
    v = iv.astype(f32).reshape(bsz, t_len, C_HEADS, C_VDIM)
    c = min(CHUNK, t_len)
    n_chunks = -(-t_len // c)
    pad = n_chunks * c - t_len

    def to_chunks(z):
        z = jnp.pad(z, ((0, 0), (0, pad), (0, 0), (0, 0)))
        return z.reshape(bsz, n_chunks, c, C_HEADS, -1).transpose(1, 0, 3, 2, 4)

    mask = jnp.tril(jnp.ones((c, c), dtype=bool))

    def step(s, inp):
        q_c, lf_c, k_c, v_c = inp
        g_cum = jnp.cumsum(lf_c, axis=2)
        o_inter = jnp.einsum('bhtk,bhkv->bhtv', q_c * jnp.exp(g_cum), s)
        diff = g_cum[:, :, :, None, :] - g_cum[:, :, None, :, :]
        dec = jnp.exp(jnp.where(mask[:, :, None], diff, -jnp.inf))
        att = jnp.einsum('bhtk,bhsk,bhtsk->bhts', q_c, k_c, dec)
        o = o_inter + jnp.einsum('bhts,bhsv->bhtv', att, v_c)
        g_last = g_cum[:, :, -1:, :]
        s = jnp.exp(g_last)[:, :, 0, :, None] * s + jnp.einsum('bhsk,bhsv->bhkv', k_c * jnp.exp(g_last - g_cum), v_c)
        return s, o

    s_last, o = lax.scan(step, s0.astype(f32), tuple(to_chunks(z) for z in (q, logf, k, v)))
    o = o.transpose(1, 0, 3, 2, 4).reshape(bsz, n_chunks * c, C_HEADS, C_VDIM)[:, :t_len]
    o = o * lax.rsqrt(jnp.mean(o * o, axis=-1, keepdims=True) + RMS_EPS) * norm_g.astype(f32).reshape(C_HEADS, C_VDIM)
    out = (o.reshape(bsz, t_len, C_WIDTH) * jax.nn.silu(gz.astype(f32))).astype(p.dtype)
    return out, s_last

def token_mix(u, l, P, lb_l, s_rwkv, s_shift, s_lru, s_conv, s_hgrn):
    proj = u @ P['w_in'][l]
    pa, pb, pc, pg = jnp.split(proj, [A_PROJ, A_PROJ + 2 * B_WIDTH, A_PROJ + 2 * B_WIDTH + 2 * C_KWIDTH + 2 * C_WIDTH], axis=-1)
    oa, n_shift, n_rwkv = rwkv7_mixer(pa, s_shift, s_rwkv, P['rwkv_mu'][l], P['rwkv_w0'][l], P['rwkv_w2'][l], P['rwkv_a0'][l], P['rwkv_a2'][l], P['rwkv_g2'][l], P['rwkv_k_k'][l], P['rwkv_k_a'][l], P['rwkv_r_k'][l], P['rwkv_ln_g'][l], P['rwkv_ln_b'][l])
    ob, n_conv, n_lru = rglru_mixer(pb, s_conv, s_lru, P['lru_conv_w'][l], P['lru_conv_b'][l], P['lru_wa'][l], P['lru_ba'][l], P['lru_wx'][l], P['lru_bx'][l], P['lru_lam'][l])
    oc, n_hgrn = hgrn2_mixer(pc, s_hgrn, lb_l, P['hgrn_norm_g'][l])
    ga, gb, gc = jnp.split(jax.nn.sigmoid(pg), 3, axis=-1)
    merged = ga * (oa @ P['proj_a'][l]) + gb * (ob @ P['proj_b'][l]) + gc * (oc @ P['proj_c'][l])
    return merged @ P['w_out'][l], (n_rwkv, n_shift, n_lru, n_conv, n_hgrn)

def run_trunk(x, s_rwkv, s_shift, s_lru, s_conv, s_hgrn, P, lb):
    collected = ([], [], [], [], [])
    for l in range(DEPTH):
        h = swiglu(rmsnorm(x, P['ffn1_pre_g'][l]), P['ffn1_wg'][l], P['ffn1_wu'][l], P['ffn1_wd'][l])
        x = x + 0.5 * rmsnorm(h, P['ffn1_post_g'][l])
        m, new = token_mix(rmsnorm(x, P['mix_pre_g'][l]), l, P, lb[l], s_rwkv[l], s_shift[l], s_lru[l], s_conv[l], s_hgrn[l])
        x = x + rmsnorm(m, P['mix_post_g'][l])
        h = swiglu(rmsnorm(x, P['ffn2_pre_g'][l]), P['ffn2_wg'][l], P['ffn2_wu'][l], P['ffn2_wd'][l])
        x = x + 0.5 * rmsnorm(h, P['ffn2_post_g'][l])
        for lst, t in zip(collected, new):
            lst.append(t)
    dt = s_rwkv.dtype
    return x, tuple(jnp.stack(lst, axis=0).astype(dt) for lst in collected)

def setup_inputs(seed: int = 0) -> dict:
    key = jax.random.key(seed)
    ks = iter(jax.random.split(key, 80))
    f32 = jnp.float32

    def nrm(shape, scale):
        return scale * jax.random.normal(next(ks), shape, f32)

    def gain(shape):
        return 1.0 + nrm(shape, 0.05)

    def unif(shape, lo, hi):
        return jax.random.uniform(next(ks), shape, f32, lo, hi)

    D, L = D_MODEL, DEPTH
    inp = {}
    inp['x_prompt'] = nrm((BATCH, SEQ, D), 1.0)
    inp['x_sample'] = nrm((DEC_BATCH, DEC_SEQ, D), 1.0)
    inp['state_rwkv'] = nrm((L, DEC_BATCH, A_HEADS, A_HEAD_DIM, A_HEAD_DIM), 0.1)
    inp['state_shift'] = nrm((L, DEC_BATCH, A_PROJ), 1.0)
    inp['state_lru'] = nrm((L, DEC_BATCH, B_WIDTH), 0.5)
    inp['state_conv'] = nrm((L, DEC_BATCH, CONV_W - 1, B_WIDTH), 1.0)
    inp['state_hgrn'] = nrm((L, DEC_BATCH, C_HEADS, C_KDIM, C_VDIM), 0.5)
    inp['ffn1_pre_g'] = gain((L, D))
    inp['ffn1_post_g'] = gain((L, D))
    inp['ffn1_wg'] = nrm((L, D, D_FF), D ** -0.5)
    inp['ffn1_wu'] = nrm((L, D, D_FF), D ** -0.5)
    inp['ffn1_wd'] = nrm((L, D_FF, D), D_FF ** -0.5)
    inp['mix_pre_g'] = gain((L, D))
    inp['mix_post_g'] = gain((L, D))
    inp['w_in'] = nrm((L, D, N_IN), D ** -0.5)
    inp['rwkv_mu'] = unif((L, A_PROJ), 0.0, 1.0)
    inp['rwkv_w0'] = nrm((L, A_WIDTH), 0.5)
    inp['rwkv_w2'] = nrm((L, DECAY_LORA, A_WIDTH), 0.1)
    inp['rwkv_a0'] = nrm((L, A_WIDTH), 0.1)
    inp['rwkv_a2'] = nrm((L, AAA_LORA, A_WIDTH), 0.1)
    inp['rwkv_g2'] = nrm((L, GATE_LORA, A_WIDTH), GATE_LORA ** -0.5)
    inp['rwkv_k_k'] = 0.85 + nrm((L, A_WIDTH), 0.05)
    inp['rwkv_k_a'] = gain((L, A_WIDTH))
    inp['rwkv_r_k'] = nrm((L, A_HEADS, A_HEAD_DIM), 0.1)
    inp['rwkv_ln_g'] = gain((L, A_WIDTH))
    inp['rwkv_ln_b'] = nrm((L, A_WIDTH), 0.02)
    inp['lru_conv_w'] = nrm((L, CONV_W, B_WIDTH), 0.5)
    inp['lru_conv_b'] = nrm((L, B_WIDTH), 0.02)
    inp['lru_wa'] = nrm((L, B_BLOCKS, B_BLOCK, B_BLOCK), B_BLOCK ** -0.5)
    inp['lru_ba'] = nrm((L, B_WIDTH), 0.02)
    inp['lru_wx'] = nrm((L, B_BLOCKS, B_BLOCK, B_BLOCK), B_BLOCK ** -0.5)
    inp['lru_bx'] = nrm((L, B_WIDTH), 0.02)
    inp['lru_lam'] = unif((L, B_WIDTH), 2.0, 6.0)
    inp['hgrn_lb_logits'] = nrm((L, C_KWIDTH), 1.0)
    inp['hgrn_norm_g'] = gain((L, C_WIDTH))
    inp['proj_a'] = nrm((L, A_WIDTH, D), A_WIDTH ** -0.5)
    inp['proj_b'] = nrm((L, B_WIDTH, D), B_WIDTH ** -0.5)
    inp['proj_c'] = nrm((L, C_WIDTH, D), C_WIDTH ** -0.5)
    inp['w_out'] = nrm((L, D, D), D ** -0.5)
    inp['ffn2_pre_g'] = gain((L, D))
    inp['ffn2_post_g'] = gain((L, D))
    inp['ffn2_wg'] = nrm((L, D, D_FF), D ** -0.5)
    inp['ffn2_wu'] = nrm((L, D, D_FF), D ** -0.5)
    inp['ffn2_wd'] = nrm((L, D_FF, D), D_FF ** -0.5)
    return inp

def reference(x_prompt, x_sample, state_rwkv, state_shift, state_lru, state_conv, state_hgrn,
              ffn1_pre_g, ffn1_post_g, ffn1_wg, ffn1_wu, ffn1_wd,
              mix_pre_g, mix_post_g, w_in,
              rwkv_mu, rwkv_w0, rwkv_w2, rwkv_a0, rwkv_a2, rwkv_g2, rwkv_k_k, rwkv_k_a, rwkv_r_k, rwkv_ln_g, rwkv_ln_b,
              lru_conv_w, lru_conv_b, lru_wa, lru_ba, lru_wx, lru_bx, lru_lam,
              hgrn_lb_logits, hgrn_norm_g,
              proj_a, proj_b, proj_c, w_out,
              ffn2_pre_g, ffn2_post_g, ffn2_wg, ffn2_wu, ffn2_wd):
    P = {
        'ffn1_pre_g': ffn1_pre_g, 'ffn1_post_g': ffn1_post_g, 'ffn1_wg': ffn1_wg, 'ffn1_wu': ffn1_wu, 'ffn1_wd': ffn1_wd,
        'mix_pre_g': mix_pre_g, 'mix_post_g': mix_post_g, 'w_in': w_in,
        'rwkv_mu': rwkv_mu, 'rwkv_w0': rwkv_w0, 'rwkv_w2': rwkv_w2, 'rwkv_a0': rwkv_a0, 'rwkv_a2': rwkv_a2,
        'rwkv_g2': rwkv_g2, 'rwkv_k_k': rwkv_k_k, 'rwkv_k_a': rwkv_k_a, 'rwkv_r_k': rwkv_r_k,
        'rwkv_ln_g': rwkv_ln_g, 'rwkv_ln_b': rwkv_ln_b,
        'lru_conv_w': lru_conv_w, 'lru_conv_b': lru_conv_b, 'lru_wa': lru_wa, 'lru_ba': lru_ba,
        'lru_wx': lru_wx, 'lru_bx': lru_bx, 'lru_lam': lru_lam,
        'hgrn_norm_g': hgrn_norm_g,
        'proj_a': proj_a, 'proj_b': proj_b, 'proj_c': proj_c, 'w_out': w_out,
        'ffn2_pre_g': ffn2_pre_g, 'ffn2_post_g': ffn2_post_g, 'ffn2_wg': ffn2_wg, 'ffn2_wu': ffn2_wu, 'ffn2_wd': ffn2_wd,
    }
    lb_cum = jnp.cumsum(jax.nn.softmax(hgrn_lb_logits.astype(jnp.float32), axis=0), axis=0)
    lb = lb_cum - lb_cum[0]
    bp = x_prompt.shape[0]
    dt = state_rwkv.dtype
    y_prompt, p_st = run_trunk(
        x_prompt,
        jnp.zeros((DEPTH, bp, A_HEADS, A_HEAD_DIM, A_HEAD_DIM), dt),
        jnp.zeros((DEPTH, bp, A_PROJ), dt),
        jnp.zeros((DEPTH, bp, B_WIDTH), dt),
        jnp.zeros((DEPTH, bp, CONV_W - 1, B_WIDTH), dt),
        jnp.zeros((DEPTH, bp, C_HEADS, C_KDIM, C_VDIM), dt),
        P, lb)
    y_sample, s_st = run_trunk(x_sample, state_rwkv, state_shift, state_lru, state_conv, state_hgrn, P, lb)
    return (y_prompt, y_sample, p_st[0], p_st[1], p_st[2], p_st[3], p_st[4], s_st[0], s_st[1], s_st[2], s_st[3], s_st[4])


_drawn_inputs = setup_inputs


def setup_inputs(seed=0):
    import zlib

    import numpy as np

    out = dict(_drawn_inputs(seed))
    spreads = {}
    factors = {'rwkv_k_k': 4.31, 'lru_ba': 8.0, 'lru_bx': 7.509}
    for name, (base, spread) in spreads.items():
        noise = np.random.default_rng([zlib.crc32(name.encode()), seed]).standard_normal(out[name].shape)
        drawn = base * np.exp(spread * noise) if base else spread * noise
        out[name] = __import__('jax').numpy.asarray(drawn.astype(out[name].dtype))
    for name, factor in factors.items():
        out[name] = (out[name] * factor).astype(out[name].dtype)
    return out
```

```python
from contextlib import ExitStack

import numpy as np

import concourse.bass as bass
from concourse import mybir

F32 = mybir.dt.float32
U32 = mybir.dt.uint32
ALU = mybir.AluOpType
ACT = mybir.ActivationFunctionType
AX = mybir.AxisListType

P = 128
D = 1024
KD = D // P
L = 2
TP = 256
NB = 8
TS = 8
T = TP + NB * TS
DFF = 2816
KF = DFF // P
CH = 64
NCH = T // CH
HP = 4
BLK = 2048
EPS = 1e-6
GN_EPS = 64e-5
EM05 = float(np.exp(-0.5))

B_F1, B_A, B_B, B_C, B_G0, B_G1, B_PROJ, B_OUT, B_F2, NBLK = 0, 34, 42, 46, 54, 58, 66, 72, 76, 110
Q_F1, Q_A, Q_B, Q_C, Q_G0, Q_G1, Q_PROJ, Q_OUT, Q_F2, NPAIR = 0, 26, 34, 38, 46, 50, 58, 70, 74, 100

PARAMS = [("ffn1_pre_g", 8), ("ffn1_post_g", 8), ("mix_pre_g", 8), ("mix_post_g", 8), ("ffn2_pre_g", 8),
          ("ffn2_post_g", 8), ("rwkv_mu", 14), ("rwkv_w0", 4), ("rwkv_a0", 4), ("rwkv_k_k", 4), ("rwkv_k_a", 4),
          ("rwkv_r_k", 4), ("rwkv_ln_g", 4), ("rwkv_ln_b", 4), ("lru_conv_w", 16), ("lru_conv_b", 4),
          ("lru_ba", 4), ("lru_bx", 4), ("lru_lam", 4), ("hgrn_norm_g", 4)]
PCOL = {}
_n = 0
for _name, _w in PARAMS:
    PCOL[_name] = _n
    _n += _w
NPARAM = _n


def constants():
    i = np.arange(P)
    s, t = i[:, None], i[None, :]
    head = (s // CH) == (t // CH)
    batch = (s // TS) == (t // TS)
    parts = {
        "ident": s == t,
        "ones": np.ones((P, P)),
        "blk": head,
        "istack": (s % CH) == np.arange(CH)[None, :],
        "mask_p": np.concatenate([head & (s < t), head & (s <= t)], 1),
        "mask_s": np.concatenate([batch & (s < t), batch & (s <= t)], 1),
        "level": np.concatenate([((s // (2 * h)) == (t // (2 * h))) & (s % (2 * h) < h) & (t % (2 * h) >= h)
                                 for h in (1, 2, 4, 8, 16, 32, 64)], 1),
        "mask_b": ((s % CH) // TS) == np.arange(NB)[None, :],
    }
    tok = np.arange(T)
    seg_a = np.where(tok < TP, tok % CH != 0, tok % TS != 0)
    seg_b = np.where(tok < TP, tok != 0, tok % TS != 0)
    parts["seg_a"] = np.broadcast_to(seg_a, (P, T))
    parts["seg_b"] = np.broadcast_to(seg_b, (P, T))
    at, n = {}, 0
    for k, v in parts.items():
        at[k] = (n, v.shape[1])
        n += v.shape[1]
    return np.concatenate([v.astype(np.float32) for v in parts.values()], 1), at


CONST_AT = constants()[1]
NCONST = sum(w for _, w in CONST_AT.values())


def trunk(nc, xT, wstream, smallw, params, logits, consts, st_shift, st_rwkv, st_lru, st_conv, st_hgrn,
          yT, o_shift, o_rwkv, o_lru, o_conv, o_hgrn):
    ctx = ExitStack()
    with ctx:
        def sb(name, *shape):
            return ctx.enter_context(nc.sbuf_tensor(name, [P, *shape], F32))

        def sem(name):
            return ctx.enter_context(nc.semaphore(name))

        cst = sb("cst", NCONST)

        def const(name, *shape):
            a, w = CONST_AT[name]
            v = cst[:, a:a + w]
            return v.rearrange("p (a b) -> p a b", a=shape[0]) if shape else v

        ident, ones, blk, istack = const("ident"), const("ones"), const("blk"), const("istack")
        mask_p, mask_s, level = const("mask_p"), const("mask_s"), const("level", 7)
        mask_b, seg_a, seg_b = const("mask_b"), const("seg_a"), const("seg_b")
        x = sb("x", KD, T)
        u = sb("u", KD, T)
        ho = sb("ho", KD, T)
        sq = sb("sq", KD, T)
        rt = sb("rt", T)
        rs = sb("rs", T)
        raw = [sb(f"raw{i}", BLK) for i in range(2)]
        sw = sb("sw", 4, 512)
        prm = sb("prm", NPARAM)
        lg = sb("lg", L, 4)
        lbt = sb("lbt", L, 4)
        lgt = sb("lgt", 4, 4)
        lbc = sb("lbc", 2, 4)
        E = sb("E", 5, NCH, P)
        YE = sb("YE", NCH, P)
        epst = sb("epst", 2)
        pair = sb("pair", 6, T)
        zs = sb("zs", NCH, P)
        btok = sb("btok", NCH, P)
        ktok = sb("ktok", NCH, P)
        vtok = sb("vtok", NCH, CH)
        st = sb("st", NCH, CH)
        stg = sb("stg", CH)
        pn = sb("pn", CH)
        uu = sb("uu", CH)
        ps1 = sb("ps1", CH)
        ss = sb("ss", NB, CH)
        ssn = sb("ssn", NB, CH)
        hs = sb("hs", NB, P)
        hsn = sb("hsn", NB, P)
        shift_in = sb("shift_in", 14, NB)
        shift_out = sb("shift_out", 14, NB + 1)
        lru_in = sb("lru_in", 4, NB)
        lru_out = sb("lru_out", 4, NB + 1)
        conv_in = sb("conv_in", 4, NB, 3)
        conv_out = sb("conv_out", 4, NB + 1, 3)
        spc = sb("spc", 6, 4)

        ov = sb("ov", 64, T)
        hff, gs = ov[:, 0:KF, :], ov[:, KF:KF + 2, :]
        gate, pbc, oa, lo = ov[:, 0:24, :], ov[:, 24:48, :], ov[:, 48:52, :], ov[:, 52:64, :]
        ob, oc = pbc[:, 0:4, :], pbc[:, 8:12, :]
        pa = gate[:, 0:14, :]
        logd, cum, cumm, kk0, kp, bb, gam, igam, gamm, rkv = (gate[:, 14 + i, :] for i in range(10))
        xs, dd = pair[:, 0:3, :], pair[:, 3:6, :]
        kksq, rkr, nrm = (dd[:, i, :] for i in range(3))
        sqf = sq[:, :, :].rearrange("p a t -> p (a t)")
        hof = ho[:, :, :].rearrange("p a t -> p (a t)")

        def chunks(v):
            return v.rearrange("p (c s) -> p c s", c=NCH)

        abq = sqf.rearrange("p (c k s) -> p c k s", c=NCH, k=4)
        ao = [chunks(hof[:, 640 * i:640 * (i + 1)]) for i in range(2)]
        tinv, tinvt = chunks(hof[:, 1280:1920]), chunks(hof[:, 1920:2560])

        def streams(v):
            return v.rearrange("p (b v) -> p b v", b=NB)

        ub = streams(zs[:, :, :].rearrange("p c s -> p (c s)")[:, 0:512])
        vb, tmpb = streams(hof[:, 0:512]), streams(hof[:, 640:1152])
        hq, hf, hk = xs[:, 0, :], xs[:, 1, :], xs[:, 2, :]
        pre, suf, gzs = dd[:, 0, :], dd[:, 1, :], dd[:, 2, :]
        qp, ks, att, sgq, sgf, sgz, osb, osq = (ho[:, i, :] for i in range(8))
        vt3 = sqf[:, 0:384].rearrange("p (c v) -> p c v", c=3)
        kt3 = sqf[:, 384:768].rearrange("p (c v) -> p c v", c=3)
        hvb = streams(sqf[:, 768:1792])
        hst = sqf[:, 1792:2048].rearrange("p (b v) -> p b v", b=2)
        hv = ktok[:, :, :].rearrange("p c s -> p (c s)")[:, 0:T]
        hrt = zs[:, :, :].rearrange("p c s -> p (c s)")[:, 0:T]
        hrs = btok[:, :, :].rearrange("p c s -> p (c s)")[:, 0:T]
        XPW = 3 + TP + NB * (3 + TS)
        xp = pair[:, :, :].rearrange("p a t -> p (a t)")[:, 0:4 * XPW].rearrange("p (k n) -> p k n", k=4)
        xc, lr, li, la = sq[:, 0:4, :], sq[:, 4:8, :], ho[:, 0:4, :], ho[:, 4:8, :]
        lth, lb_, lge = lo[:, 0:4, :], lo[:, 4:8, :], lo[:, 8:12, :]
        merged = sq

        dps = ctx.enter_context(nc.psum_tensor("dps", [P, 4, 512], F32))
        mx = ctx.enter_context(nc.psum_tensor("mx", [P, 4, 512], F32))
        mx01 = mx[:, 0:2, :].rearrange("p b n -> p (b n)")
        mx23 = mx[:, 2:4, :].rearrange("p b n -> p (b n)")

        names = """const_loaded x_loaded prm_loaded shift_loaded lru_loaded ss_loaded hs_loaded
        block_done proj_half x_new sq_ready sum_done rt_ready u_ready silu_ready h_ready
        lgexp_in lgexp_out zero_ready eps_ready pa_ready pbc_ready lora_in_ready lora_act_ready lora_done lora_ready
        kk0_ready kksq_ready kn_done norm_ready rkr_ready rk_done cum_ready cumm_ready gam_ready xs_ready ve_ready
        e_ready abq_done abq_ready tok_done tok_ready ao_ready z_done z_ready pt_done t_ready
        p_done pn_ready u_done uc_ready s_done s_ready y_done ye_ready sp_done spn_ready sr_done sy_done su_done
        suc_ready sst_done ye4_ready yt_done yt_ready mean_done dev_ready devsq_ready var_done sd_ready oa_ready
        ss_stored ssn_ready shift_stored shift_out_ready
        xc_ready lg_done lgate_ready spln_ready lam_ready a_ready b2_ready bs_ready ob_ready
        lru_out_ready lru_stored
        hsig_ready hq_ready att_done qk_ready ht_done ht_ready hkt_ready hst1_done hst1_ready
        hb_ready hst_done o_done osq_ready om_done osd_ready oc_ready hs_stored hsn_ready
        merged_ready y_stored shift_free lru_free ss_free hs_free""".split()
        S = {n: sem(n) for n in names}
        w_loaded = [sem("w_loaded0"), sem("w_loaded1")]
        pair_free = [sem("pair_free0"), sem("pair_free1")]

        def pcol(name, i, n=1):
            a = PCOL[name]
            return prm[:, a + i:a + i + n] if isinstance(i, int) else prm[:, bass.ds(i + a, n)]

        def tiles_at(t, i, n):
            return t[:, i:i + n, :] if isinstance(i, int) else t[:, bass.ds(i, n), :]

        def tile_at(t, i):
            return t[:, i, :] if isinstance(i, int) else t[:, bass.ds(i, 1), :].rearrange("p a t -> p (a t)")

        def wait_block(eng, l, j):
            eng.wait_ge(S["block_done"], l * NBLK + (j + 3))

        def wait_apart(eng, name, value):
            value = eng.to_reg(value)
            eng.wait_ge(S["const_loaded"], 32)
            eng.wait_ge(S[name], value)

        block = ctx.enter_context(nc.Block())

        @block.sync
        def _(sp):
            sp.dma_start(x[:, :, :], xT).then_inc(S["x_loaded"], 16)
            with sp.Fori(0, L * NBLK // 2) as i:
                for s in range(2):
                    sp.wait_ge(S["block_done"], i * 2 + (s + 1))
                    sp.dma_start(raw[s][:, :], wstream[bass.ds(i * 2 + s, 1), :, :]
                                 .rearrange("a p n -> (a p) n")).then_inc(w_loaded[s], 16)
            sp.wait_ge(S["x_new"], 3 * L + 1)
            sp.dma_start(yT, x[:, :, :]).then_inc(S["y_stored"], 16)
            sp.wait_ge(S["y_stored"], 16)

        @block.gpsimd
        def _(pool):
            pool.dma_start(cst[:, :], consts).then_inc(S["const_loaded"], 16)
            pool.dma_start(lg[:, :, :], logits).then_inc(S["const_loaded"], 16)
            for free in ("shift_free", "lru_free", "ss_free", "hs_free"):
                pool.sem_inc(S[free], 1)
            pool.memset(E[:, :, :, :], 0.0).then_inc(S["zero_ready"], 1)
            pool.memset(YE[:, :, :], 0.0).then_inc(S["zero_ready"], 1)

            def lay(t, l):
                return t[bass.ds(l, 1)]

            with pool.Fori(0, L) as l:
                wait_apart(pool, "x_new", l * 3 + 1)
                pool.dma_start(prm[:, :], lay(params, l).rearrange("a p n -> (a p) n")).then_inc(S["prm_loaded"], 16)
                pool.dma_start(sw[:, :, :], lay(smallw, l).rearrange("a p k n -> (a p) k n"))\
                    .then_inc(S["prm_loaded"], 16)
                pool.dma_start(shift_in[:, :, :], lay(st_shift, l).rearrange("a p k n -> (a p) k n"))\
                    .then_inc(S["shift_loaded"], 16)
                pool.dma_start(lru_in[:, :, :], lay(st_lru, l).rearrange("a p k n -> (a p) k n"))\
                    .then_inc(S["lru_loaded"], 16)
                pool.dma_start(conv_in[:, :, :, :].rearrange("p k b n -> p k (b n)"),
                               lay(st_conv, l).rearrange("a p k n -> (a p) k n")).then_inc(S["lru_loaded"], 16)
                wait_apart(pool, "shift_out_ready", l + 1)
                pool.dma_start(lay(o_shift, l).rearrange("a p k n -> (a p) k n"), shift_out[:, :, :])\
                    .then_inc(S["shift_stored"], 16)
                pool.wait_ge(S["shift_stored"], l * 16 + 16)
                pool.sem_inc(S["shift_free"], 1)
                with pool.Fori(0, HP) as p:
                    n = l * HP + p
                    wait_apart(pool, "oa_ready", n + 1)
                    pool.dma_start(ss[:, :, :], st_rwkv[bass.ds(n, 1)].rearrange("a p b v -> (a p) b v"))\
                        .then_inc(S["ss_loaded"], 16)
                    wait_apart(pool, "ssn_ready", n + 1)
                    pool.dma_start(o_rwkv[bass.ds(n, 1), :, 0:1, :].rearrange("a p b v -> (a p) (b v)"), st[:, 4, :])\
                        .then_inc(S["ss_stored"], 16)
                    pool.dma_start(o_rwkv[bass.ds(n, 1), :, 1:NB + 1, :].rearrange("a p b v -> (a p) b v"),
                                   ssn[:, :, :]).then_inc(S["ss_stored"], 16)
                    pool.wait_ge(S["ss_stored"], n * 32 + 32)
                    pool.sem_inc(S["ss_free"], 1)
                wait_apart(pool, "lru_out_ready", l + 1)
                pool.dma_start(lay(o_lru, l).rearrange("a p k n -> (a p) k n"), lru_out[:, :, :])\
                    .then_inc(S["lru_stored"], 16)
                pool.dma_start(lay(o_conv, l).rearrange("a p k n -> (a p) k n"),
                               conv_out[:, :, :, :].rearrange("p k b n -> p k (b n)")).then_inc(S["lru_stored"], 16)
                pool.wait_ge(S["lru_stored"], l * 32 + 32)
                pool.sem_inc(S["lru_free"], 1)
                with pool.Fori(0, 4) as p:
                    n = l * 4 + p
                    wait_apart(pool, "oc_ready", n + 1)
                    pool.dma_start(hs[:, :, :], st_hgrn[bass.ds(n, 1)].rearrange("a p b v -> (a p) b v"))\
                        .then_inc(S["hs_loaded"], 16)
                    wait_apart(pool, "hsn_ready", n + 1)
                    pool.dma_start(o_hgrn[bass.ds(n, 1), :, 0:1, :].rearrange("a p b v -> (a p) (b v)"), hst[:, 1, :])\
                        .then_inc(S["hs_stored"], 16)
                    pool.dma_start(o_hgrn[bass.ds(n, 1), :, 1:NB + 1, :].rearrange("a p b v -> (a p) b v"),
                                   hsn[:, :, :]).then_inc(S["hs_stored"], 16)
                    pool.wait_ge(S["hs_stored"], n * 32 + 32)
                    pool.sem_inc(S["hs_free"], 1)
            pool.wait_ge(S["shift_stored"], 16 * L)
            pool.wait_ge(S["lru_stored"], 32 * L)
            pool.wait_ge(S["ss_stored"], 32 * HP * L)
            pool.wait_ge(S["hs_stored"], 32 * 4 * L)

        @block.tensor
        def _(pe):
            pe.sem_inc(S["block_done"], 2)
            pe.wait_ge(S["const_loaded"], 32)
            pe.wait_ge(S["zero_ready"], 2)

            def block_in(l, half, s):
                pe.wait_ge(w_loaded[s], (l * (NBLK // 2) + half) * 16 + 16)

            def pair_wait(l, qhalf, s):
                pe.wait_ge(pair_free[s], l * (NPAIR // 2) + qhalf + 1)

            def tiles(s, kt, width, src, half, first=True, last=True, cols=(0, 1), k0=0, col0=0):
                w = raw[s][:, 0:kt * width].rearrange("p (k n) -> p k n", k=kt)
                for c in cols:
                    for k in range(kt):
                        m = pe.matmul(dps[:, 2 * half + c, 0:T], w[:, k, (col0 + c) * P:(col0 + c + 1) * P],
                                      src[:, k0 + k, :], start=first and k == 0, stop=last and k == kt - 1,
                                      skip_group_check=True)
                return m

            def norm_sum(l, idx):
                pe.wait_ge(S["sq_ready"], l * 6 + (idx + 1))
                for k in range(KD):
                    m = pe.matmul(mx[:, 3, 0:T], ones, sq[:, k, :], start=k == 0, stop=k == KD - 1)
                m.then_inc(S["sum_done"], 1)

            def dense(l, b, q, turns):
                with pe.Fori(0, turns) as i:
                    for s in range(2):
                        block_in(l, i + b // 2, s)
                        pair_wait(l, i + q // 2, s)
                        tiles(s, KD, 256, u, s).then_inc(S["block_done"], 1)

            def ffn(l, b, q, f):
                norm_sum(l, 4 * f)
                wait_apart(pe, "u_ready", l * 3 + (2 * f + 1))
                dense(l, b, q, KF // 2)
                wait_apart(pe, "h_ready", l * 22 + (11 * f + 12))
                b1, q1 = b + KF, q + KF
                with pe.Fori(0, 2) as i:
                    for j in range(6):
                        s, half, part = j % 2, j // 3, j % 3
                        block_in(l, i * 3 + (b1 // 2 + j // 2), s)
                        if part == 0:
                            pair_wait(l, i + q1 // 2, half)
                        tiles(s, 8 if part < 2 else 6, 256, hff, half, first=part == 0, last=part == 2,
                              k0=8 * part).then_inc(S["block_done"], 1)
                norm_sum(l, 4 * f + 1)

            def rwkv_pair(l, p):
                n = l * HP + p

                def filler(f):
                    s, c = f // 2, f % 2
                    if c == 0:
                        block_in(l, p + B_C // 2, s)
                        pair_wait(l, p + Q_C // 2, s)
                    m = tiles(s, KD, 256, u, s, cols=(c,))
                    if c == 1:
                        m.then_inc(S["block_done"], 1)

                pe.wait_ge(S["kksq_ready"], n + 1)
                pe.matmul(mx[:, 3, 0:T], blk, kksq, start=True, stop=True).then_inc(S["kn_done"], 1)
                pe.wait_ge(S["rkr_ready"], n + 1)
                pe.matmul(mx[:, 2, 0:T], blk, rkr, start=True, stop=True).then_inc(S["rk_done"], 1)
                filler(0)
                pe.wait_ge(S["e_ready"], n + 1)
                pe.wait_ge(S["ve_ready"], n + 1)
                for c in range(NCH):
                    if c >= 2:
                        pe.wait_ge(S["abq_ready"], n * 5 + (c - 1))
                    pe.matmul(mx[:, c % 2, 0:256], E[:, 2, c, :], E[:, 0:2, c, :], start=True, stop=True,
                              skip_group_check=True)
                    pe.matmul(mx[:, c % 2, 256:512], E[:, 3, c, :], E[:, 0:2, c, :], start=False, stop=True,
                              skip_group_check=True).then_inc(S["abq_done"], 1)
                for c in range(NCH):
                    m = pe.transpose(mx23[:, c * P:(c + 1) * P], E[:, 2, c, :], ident)
                m.then_inc(S["tok_done"], 1)
                filler(1)
                pe.wait_ge(S["abq_ready"], n * 5 + 5)
                for c in range(NCH):
                    m = pe.transpose(mx01[:, c * P:(c + 1) * P], E[:, 3, c, :], ident)
                m.then_inc(S["tok_done"], 1)
                pe.wait_ge(S["tok_ready"], n * 3 + 1)
                for c in range(NCH):
                    m = pe.matmul(mx[:, 2, c * CH:(c + 1) * CH], E[:, 4, c, :], istack, start=True, stop=True)
                m.then_inc(S["tok_done"], 1)
                pe.wait_ge(S["ao_ready"], n * 6 + 1)
                pe.wait_ge(S["tok_ready"], n * 3 + 2)
                for c in range(NCH):
                    m = pe.transpose(mx01[:, c * P:(c + 1) * P], ao[0][:, c, :], ident)
                m.then_inc(S["z_done"], 1)
                pe.wait_ge(S["tok_ready"], n * 3 + 3)
                for li in range(1, 6):
                    nch = NCH if li <= 2 else NCH - 1
                    nt = NCH if li < 2 else NCH - 1 if li < 5 else 0
                    pe.wait_ge(S["ao_ready"], n * 6 + (li + 1))
                    pe.wait_ge(S["t_ready"], n * 6 + li)
                    for c in range(nch):
                        m = pe.matmul(mx01[:, c * P:(c + 1) * P], ao[li % 2][:, c, :], tinv[:, c, :],
                                      start=True, stop=True)
                    m.then_inc(S["z_done"], 1)
                    if li in (2, 4):
                        filler(2 if li == 2 else 3)
                    pe.wait_ge(S["z_ready"], n * 5 + li)
                    for c in range(nt):
                        pe.matmul(mx23[:, c * P:(c + 1) * P], tinvt[:, c, :], zs[:, c, :], start=True, stop=True)
                    for c in range(nch):
                        m = pe.matmul(mx01[:, c * P:(c + 1) * P], zs[:, c, :], tinvt[:, c, :], start=True, stop=True)
                    m.then_inc(S["pt_done"], 1)
                pe.wait_ge(S["t_ready"], n * 6 + 6)
                aE, rE = E[:, 0, :, :], E[:, 1, :, :]
                for c in range(NCH - 1):
                    pe.matmul(mx[:, 0, 0:CH], abq[:, c, 2, :], vtok[:, c, :], start=True, stop=c == 0)\
                        .then_inc(S["p_done"], 1) if c == 0 else \
                        pe.matmul(mx[:, 0, 0:CH], abq[:, c, 2, :], vtok[:, c, :], start=True, stop=False)
                    if c > 0:
                        pe.wait_ge(S["s_ready"], n * 4 + c)
                        pe.matmul(mx[:, 0, 0:CH], aE[:, c, :], st[:, c, :], start=False, stop=True)\
                            .then_inc(S["p_done"], 1)
                    pe.wait_ge(S["pn_ready"], n * 4 + (c + 1))
                    pe.matmul(mx[:, 1, 0:CH], tinvt[:, c, :], pn[:, :], start=True, stop=True).then_inc(S["u_done"], 1)
                    pe.wait_ge(S["uc_ready"], n * 4 + (c + 1))
                    pe.matmul(mx[:, 3, 0:CH], btok[:, c, :], uu[:, :], start=True, stop=False)
                    pe.matmul(mx[:, 3, 0:CH], ktok[:, c, :], vtok[:, c, :], start=False, stop=True)\
                        .then_inc(S["s_done"], 1)
                    yc = mx[:, 2, c * CH:(c + 1) * CH]
                    if c > 0:
                        pe.matmul(yc, rE[:, c, :], st[:, c, :], start=True, stop=False)
                    pe.matmul(yc, abq[:, c, 1, :], uu[:, :], start=c == 0, stop=False)
                    m = pe.matmul(yc, abq[:, c, 3, :], vtok[:, c, :], start=False, stop=True)
                m.then_inc(S["y_done"], 1)
                c = NCH - 1
                ssf = ss[:, :, :].rearrange("p b v -> p (b v)")
                pe.wait_ge(S["ss_loaded"], n * 16 + 16)
                pe.matmul(mx[:, 0, :], aE[:, c, :], ssf, start=True, stop=True)
                pe.matmul(mx[:, 1, 0:CH], abq[:, c, 2, :], vtok[:, c, :], start=True, stop=True)\
                    .then_inc(S["sp_done"], 1)
                pe.wait_ge(S["ye_ready"], n + 1)
                pe.matmul(mx[:, 2, :], rE[:, c, :], ssf, start=True, stop=True)
                pe.wait_ge(S["spn_ready"], n + 1)
                pe.matmul(mx[:, 0, 0:CH], tinvt[:, c, :], pn[:, :], start=True, stop=True).then_inc(S["su_done"], 1)
                pe.wait_ge(S["suc_ready"], n + 1)
                pe.matmul(mx[:, 3, 0:CH], abq[:, c, 1, :], uu[:, :], start=True, stop=False)
                pe.matmul(mx[:, 3, 0:CH], abq[:, c, 3, :], vtok[:, c, :], start=False, stop=True)\
                    .then_inc(S["sy_done"], 1)
                pe.matmul(mx[:, 0, :], btok[:, c, :], ub.rearrange("p b v -> p (b v)"), start=True, stop=False)
                pe.matmul(mx[:, 0, :], ktok[:, c, :], vb.rearrange("p b v -> p (b v)"), start=False, stop=True)\
                    .then_inc(S["sst_done"], 1)
                pe.wait_ge(S["ye4_ready"], n + 1)
                for c in range(NCH):
                    m = pe.matmul(mx[:, 1, c * CH:(c + 1) * CH], YE[:, c, :], istack, start=True, stop=True)
                m.then_inc(S["yt_done"], 1)
                pe.wait_ge(S["yt_ready"], n + 1)
                pe.matmul(mx[:, 2, 0:T], blk, logd, start=True, stop=True).then_inc(S["mean_done"], 1)
                pe.wait_ge(S["devsq_ready"], n + 1)
                pe.matmul(mx[:, 3, 0:T], blk, cumm, start=True, stop=True).then_inc(S["var_done"], 1)

            def hgrn_head(l, p):
                n = l * 4 + p
                SPAN = [(0, P), (P, 2 * P), (2 * P, T)]

                def filler(f):
                    s, c = f // 2, f % 2
                    if c == 0:
                        block_in(l, p + B_G1 // 2, s)
                        pair_wait(l, p + Q_G1 // 2, s)
                    m = tiles(s, KD, 256, u, s, cols=(c,))
                    if c == 1:
                        m.then_inc(S["block_done"], 1)

                pe.wait_ge(S["hsig_ready"], n + 1)
                for c, (a, b) in enumerate(SPAN):
                    m = pe.transpose(mx[0:b - a, 2, c * P:(c + 1) * P], hv[:, a:b], ident)
                m.then_inc(S["ht_done"], 1)
                filler(0)
                pe.wait_ge(S["hq_ready"], n + 1)
                for a, b in SPAN:
                    m = pe.matmul(mx[0:b - a, 0, a:b], hk[:, a:b], hq[:, a:b], start=True, stop=True)
                m.then_inc(S["att_done"], 1)
                for li in range(7):
                    pe.wait_ge(S["qk_ready"], n * 7 + (li + 1))
                    for a, b in SPAN if li < 3 else SPAN[:2]:
                        m = pe.matmul(mx[0:b - a, (li + 1) % 2, a:b], ks[:, a:b], qp[:, a:b], start=True, stop=True)
                    m.then_inc(S["att_done"], 1)
                    if li in (0, 2, 4):
                        filler(1 + li // 2)
                pe.wait_ge(S["hkt_ready"], n + 1)
                for c, (a, b) in enumerate(SPAN):
                    m = pe.transpose(mx[0:b - a, 3, c * P:(c + 1) * P], ks[:, a:b], ident)
                m.then_inc(S["ht_done"], 1)
                pe.wait_ge(S["ht_ready"], n * 2 + 2)
                pe.matmul(mx[:, 2, 0:P], kt3[:, 0, :], vt3[:, 0, :], start=True, stop=True)
                pe.matmul(mx[:, 2, P:2 * P], kt3[:, 1, :], vt3[:, 1, :], start=True, stop=True)\
                    .then_inc(S["hst1_done"], 1)
                pe.wait_ge(S["hb_ready"], n + 1)
                for j in range(2):
                    m = pe.matmul(mx[:, j, :], kt3[0:CH, 2, :], hvb[0:CH, 4 * j:4 * j + 4, :], start=True, stop=True)
                m.then_inc(S["hst_done"], 1)
                pe.wait_ge(S["hst1_ready"], n + 1)
                pe.wait_ge(S["hs_loaded"], n * 16 + 16)
                pe.matmul(mx[:, 3, 0:P], vt3[:, 0, :], att[:, 0:P], start=True, stop=True)
                pe.matmul(mx[:, 3, P:2 * P], vt3[:, 1, :], att[:, P:2 * P], start=True, stop=False)
                pe.matmul(mx[:, 3, P:2 * P], hst[:, 0, :], qp[:, P:2 * P], start=False, stop=True)
                pe.matmul(mx[:, 3, 2 * P:T], vt3[0:CH, 2, :], att[0:CH, 2 * P:T], start=True, stop=False)
                for b in range(NB):
                    t0 = TP + b * TS
                    m = pe.matmul(mx[:, 3, t0:t0 + TS], hs[:, b, :], qp[:, t0:t0 + TS], start=False, stop=b == NB - 1)
                m.then_inc(S["o_done"], 1)
                pe.wait_ge(S["osq_ready"], n + 1)
                pe.matmul(mx[:, 2, 0:T], ones, osq, start=True, stop=True).then_inc(S["om_done"], 1)

            with pe.Fori(0, L) as l:
                pe.wait_ge(S["prm_loaded"], l * 32 + 32)
                ffn(l, B_F1, Q_F1, 0)
                norm_sum(l, 2)
                wait_apart(pe, "u_ready", l * 3 + 2)
                dense(l, B_A, Q_A, 3)
                for s in range(2):
                    block_in(l, B_A // 2 + 3, s)
                    pair_wait(l, Q_A // 2 + 3, s)
                    tiles(s, KD, P, u, s, cols=(0,)).then_inc(S["block_done"], 1)
                dense(l, B_B, Q_B, 1)
                pe.wait_ge(S["lora_act_ready"], l + 1)
                for kind in range(3):
                    if kind:
                        pe.wait_ge(S["lora_ready"], l * 3 + kind)
                    a, b, which = ((0, CH, 0), (CH, P, 0), (0, P, 1))[kind]
                    src = kp if kind == 2 else bb
                    for j in range(4):
                        m = pe.matmul(mx[:, j, 0:T], sw[a:b, which, j * P:(j + 1) * P], src[a:b, :], start=True, stop=True)
                    m.then_inc(S["lora_done"], 1)
                dense(l, B_B + 2, Q_B + 2, 1)
                with pe.Fori(0, HP) as p:
                    rwkv_pair(l, p)
                dense(l, B_G0, Q_G0, 1)
                pe.wait_ge(S["xc_ready"], l + 1)
                for kind in range(2):
                    if kind:
                        pe.wait_ge(S["lgate_ready"], l * 2 + 1)
                    for j in range(4):
                        m = pe.matmul(mx[:, j, 0:T], sw[:, 2 + kind, j * P:(j + 1) * P], xc[:, j, :], start=True, stop=True)
                    m.then_inc(S["lg_done"], 1)
                dense(l, B_G0 + 2, Q_G0 + 2, 1)
                with pe.Fori(0, 4) as p:
                    hgrn_head(l, p)
                pe.wait_ge(S["ob_ready"], l + 1)
                pe.wait_ge(S["oc_ready"], l * 4 + 5)
                for br, src in enumerate((oa, ob, oc)):
                    for s in range(2):
                        block_in(l, B_PROJ // 2 + br, s)
                        for half in range(2):
                            pair_wait(l, (Q_PROJ + 4 * br + 2 * s) // 2, half)
                            m = tiles(s, 4, 512, src, half, col0=2 * half)
                            m.then_inc(S["block_done"] if half else S["proj_half"], 1)
                wait_apart(pe, "merged_ready", l + 1)
                with pe.Fori(0, 2) as i:
                    for s in range(2):
                        block_in(l, i + B_OUT // 2, s)
                        pair_wait(l, i + Q_OUT // 2, s)
                        tiles(s, KD, 256, merged, s).then_inc(S["block_done"], 1)
                norm_sum(l, 3)
                ffn(l, B_F2, Q_F2, 1)

        @block.scalar
        def _(act):
            def fn(out, in_, f, **kw):
                return nc.scalar.activation(out, in_, f, **kw)

            act.wait_ge(S["const_loaded"], 32)
            act.wait_ge(S["zero_ready"], 2)
            act.wait_ge(S["eps_ready"], 2)
            act.wait_ge(S["x_loaded"], 16)
            act.wait_ge(S["lgexp_in"], 1)
            fn(lgt[:, 2:4, :], lgt[:, 0:2, :], ACT.Exp).then_inc(S["lgexp_out"], 1)

            def norm(l, idx, src):
                if idx % 2 == 0:
                    act.wait_ge(S["x_new"], l * 3 + (idx // 2 + 1))
                else:
                    act.drain()
                fn(sq[:, :, :], src[:, :, :], ACT.Square).then_inc(S["sq_ready"], 1)
                act.wait_ge(S["sum_done"], l * 6 + (idx + 1))
                fn(rt[:, :], mx[:, 3, 0:T], ACT.Sqrt, scale=1.0 / D, bias=epst[:, 0:1]).then_inc(S["rt_ready"], 1)

            def read_pair(l, j, s, dst, f, n=2):
                wait_block(act, l, j)
                return fn(dst, dps[:, 2 * s:2 * s + n, 0:T], f)

            def ffn(l, b, f):
                norm(l, 4 * f, x)
                with act.Fori(0, KF // 2) as i:
                    act.wait_ge(S["h_ready"], l * 22 + i + (11 * f + 1))
                    read_pair(l, i * 2 + b, 0, gs[:, :, :], ACT.Silu).then_inc(pair_free[0], 1)
                with act.Fori(0, 2) as i:
                    for h in range(2):
                        read_pair(l, i * 6 + (b + KF + 3 * h + 2), h, tiles_at(ho, i * 4 + 2 * h, 2), ACT.Copy)\
                            .then_inc(pair_free[h], 1)
                norm(l, 4 * f + 1, ho)

            def rwkv_pair(l, p):
                n = l * HP + p
                act.wait_ge(S["kk0_ready"], n + 1)
                fn(kksq, kk0, ACT.Square).then_inc(S["kksq_ready"], 1)
                act.wait_ge(S["cumm_ready"], n + 1)
                fn(gam, cum, ACT.Exp)
                fn(igam, cum, ACT.Exp, scale=-1.0)
                fn(gamm, cumm, ACT.Exp).then_inc(S["gam_ready"], 1)
                for h in range(2):
                    r = slice(CH * h, CH * h + CH)
                    m = fn(E[r, 4, :, r], chunks(xs[r, 2, :]), ACT.Copy)
                m.then_inc(S["ve_ready"], 1)
                act.wait_ge(S["kn_done"], n + 1)
                fn(nrm, mx[:, 3, 0:T], ACT.Sqrt).then_inc(S["norm_ready"], 1)
                act.wait_ge(S["tok_done"], n * 3 + 1)
                fn(btok[:, :, :], chunks(mx23[:, 0:640]), ACT.Copy).then_inc(S["tok_ready"], 1)
                read_pair(l, p * 2 + B_C, 0, tiles_at(pbc, p * 4 + 8, 2), ACT.Copy).then_inc(pair_free[0], 1)
                act.wait_ge(S["tok_done"], n * 3 + 2)
                fn(ktok[:, :, :], chunks(mx01[:, 0:640]), ACT.Copy).then_inc(S["tok_ready"], 1)
                act.wait_ge(S["tok_done"], n * 3 + 3)
                fn(vtok[:, :, :], chunks(mx[:, 2, 0:T]), ACT.Copy).then_inc(S["tok_ready"], 1)
                for li in range(1, 6):
                    nch = NCH if li <= 2 else NCH - 1
                    act.wait_ge(S["z_done"], n * 6 + (li + 1))
                    fn(zs[:, 0:nch, :], mx01[:, 0:nch * P].rearrange("p (c s) -> p c s", c=nch), ACT.Copy)\
                        .then_inc(S["z_ready"], 1)
                    if li == 4:
                        read_pair(l, p * 2 + (B_C + 1), 1, tiles_at(pbc, p * 4 + 10, 2), ACT.Copy)\
                            .then_inc(pair_free[1], 1)
                act.wait_ge(S["yt_done"], n + 1)
                fn(logd, mx[:, 1, 0:T], ACT.Copy).then_inc(S["yt_ready"], 1)
                act.wait_ge(S["dev_ready"], n + 1)
                fn(cumm, cum, ACT.Square).then_inc(S["devsq_ready"], 1)
                act.wait_ge(S["var_done"], n + 1)
                fn(kk0, mx[:, 3, 0:T], ACT.Sqrt, scale=1.0 / CH, bias=epst[:, 1:2]).then_inc(S["sd_ready"], 1)

            def hgrn_head(l, p):
                n = l * 4 + p
                act.wait_ge(S["oc_ready"], n + 1)
                for dst, t in ((sgq, 8), (sgf, 12), (sgz, 20)):
                    fn(dst, tile_at(pbc, p + t), ACT.Sigmoid)
                fn(hv, tile_at(pbc, p + 16), ACT.Copy).then_inc(S["hsig_ready"], 1)
                act.wait_ge(S["ht_done"], n * 2 + 1)
                fn(vt3[:, 0:2, :], mx[:, 2, 0:2 * P].rearrange("p (c v) -> p c v", c=2), ACT.Copy)
                fn(vt3[0:CH, 2, :], mx[0:CH, 2, 2 * P:3 * P], ACT.Copy).then_inc(S["ht_ready"], 1)
                read_pair(l, p * 2 + B_G1, 0, tiles_at(gate, p * 4 + 8, 2), ACT.Sigmoid).then_inc(pair_free[0], 1)
                read_pair(l, p * 2 + (B_G1 + 1), 1, tiles_at(gate, p * 4 + 10, 2), ACT.Sigmoid)\
                    .then_inc(pair_free[1], 1)
                act.wait_ge(S["ht_done"], n * 2 + 2)
                fn(kt3[:, 0:2, :], mx[:, 3, 0:2 * P].rearrange("p (c v) -> p c v", c=2), ACT.Copy)
                fn(kt3[0:CH, 2, :], mx[0:CH, 3, 2 * P:3 * P], ACT.Copy).then_inc(S["ht_ready"], 1)
                act.wait_ge(S["o_done"], n + 1)
                fn(osb, mx[:, 3, 0:T], ACT.Copy)
                fn(osq, mx[:, 3, 0:T], ACT.Square).then_inc(S["osq_ready"], 1)
                act.wait_ge(S["om_done"], n + 1)
                fn(hrt, mx[:, 2, 0:T], ACT.Sqrt, scale=1.0 / P, bias=epst[:, 0:1]).then_inc(S["osd_ready"], 1)

            with act.Fori(0, L) as l:
                act.wait_ge(S["prm_loaded"], l * 32 + 32)
                ffn(l, B_F1, 0)
                norm(l, 2, x)
                with act.Fori(0, 3) as i:
                    for s in range(2):
                        read_pair(l, i * 2 + (B_A + s), s, tiles_at(pa, i * 4 + 2 * s, 2), ACT.Copy)\
                            .then_inc(pair_free[s], 1)
                for s in range(2):
                    read_pair(l, B_A + 6 + s, s, pa[:, 12 + s:13 + s, :], ACT.Copy, n=1).then_inc(pair_free[s], 1)
                act.drain().then_inc(S["pa_ready"], 1)
                act.wait_ge(S["lora_in_ready"], l + 1)
                fn(bb[0:CH, :], xs[0:CH, 0, :], ACT.Tanh)
                fn(bb[CH:P, :], xs[CH:P, 0, :], ACT.Copy)
                fn(kp, xs[:, 1, :], ACT.Sigmoid).then_inc(S["lora_act_ready"], 1)
                for s in range(2):
                    read_pair(l, B_B + s, s, pbc[:, 2 * s:2 * s + 2, :], ACT.Copy).then_inc(pair_free[s], 1)
                for kind in range(3):
                    act.wait_ge(S["lora_done"], l * 3 + (kind + 1))
                    for j in range(4):
                        dst, src = lo[:, 4 * kind + j, :], mx[:, j, 0:T]
                        if kind < 2:
                            m = fn(dst, src, ACT.Sigmoid, bias=pcol(("rwkv_w0", "rwkv_a0")[kind], j))
                        else:
                            m = fn(dst, src, ACT.Copy)
                    m.then_inc(S["lora_ready"], 1)
                for s in range(2):
                    read_pair(l, B_B + 2 + s, s, pbc[:, 4 + 2 * s:6 + 2 * s, :], ACT.Copy).then_inc(pair_free[s], 1)
                with act.Fori(0, HP) as p:
                    rwkv_pair(l, p)
                act.drain().then_inc(S["pbc_ready"], 1)
                act.wait_ge(S["oa_ready"], l * 4 + 5)
                for s in range(2):
                    read_pair(l, B_G0 + s, s, gate[:, 2 * s:2 * s + 2, :], ACT.Sigmoid).then_inc(pair_free[s], 1)
                for kind in range(2):
                    act.wait_ge(S["lg_done"], l * 2 + (kind + 1))
                    for j in range(4):
                        m = fn((lr, li)[kind][:, j, :], mx[:, j, 0:T], ACT.Sigmoid,
                               bias=pcol(("lru_ba", "lru_bx")[kind], j))
                    m.then_inc(S["lgate_ready"], 1)
                for s in range(2):
                    read_pair(l, B_G0 + 2 + s, s, gate[:, 4 + 2 * s:6 + 2 * s, :], ACT.Sigmoid)\
                        .then_inc(pair_free[s], 1)
                fn(spc[:, 0, :], pcol("lru_lam", 0, 4), ACT.Abs)
                act.drain()
                fn(spc[:, 1, :], spc[:, 0, :], ACT.Exp, scale=-1.0)
                act.drain()
                fn(spc[:, 2, :], spc[:, 1, :], ACT.Ln, bias=1.0).then_inc(S["spln_ready"], 1)
                act.wait_ge(S["lam_ready"], l + 1)
                for j in range(4):
                    fn(la[:, j, :], lr[:, j, :], ACT.Exp, scale=spc[:, 4, j:j + 1])
                for j in range(4):
                    m = fn(lth[:, j, :], lr[:, j, :], ACT.Tanh, scale=spc[:, 5, j:j + 1])
                m.then_inc(S["a_ready"], 1)
                fn(lge, pbc[:, 4:8, :], ACT.Gelu_apprx_tanh)
                act.wait_ge(S["b2_ready"], l + 1)
                fn(lth, lb_, ACT.Sqrt).then_inc(S["bs_ready"], 1)
                act.wait_ge(S["ob_ready"], l + 1)
                with act.Fori(0, 4) as p:
                    hgrn_head(l, p)
                with act.Fori(0, 2) as i:
                    for s in range(2):
                        read_pair(l, i * 2 + (B_OUT + s), s, tiles_at(ho, i * 4 + 2 * s, 2), ACT.Copy)\
                            .then_inc(pair_free[s], 1)
                norm(l, 3, ho)
                ffn(l, B_F2, 1)

        @block.vector
        def _(dve):
            def tt(out, a, b, op):
                return nc.vector.tensor_tensor(out, a, b, op)

            def mul(out, a, b):
                return nc.vector.tensor_tensor(out, a, b, ALU.mult)

            def stt(out, in0, scalar, in1, op0, op1):
                return nc.vector.scalar_tensor_tensor(out=out, in0=in0, scalar=scalar, in1=in1, op0=op0, op1=op1)

            def ts(out, in0, s1, op0, s2=None, op1=None):
                if op1 is None:
                    return nc.vector.tensor_scalar(out, in0, s1, None, op0)
                return nc.vector.tensor_scalar(out, in0, s1, s2, op0, op1)

            fence = dve.drain

            dve.sem_inc(S["x_new"], 1)
            dve.sem_inc(S["h_ready"], 1)
            dve.sem_inc(S["oa_ready"], 1)
            dve.sem_inc(S["oc_ready"], 1)
            dve.sem_inc(pair_free[0], 1)
            dve.sem_inc(pair_free[1], 1)
            nc.vector.memset(epst[:, 0:1], EPS).then_inc(S["eps_ready"], 1)
            nc.vector.memset(epst[:, 1:2], GN_EPS).then_inc(S["eps_ready"], 1)
            dve.wait_ge(S["const_loaded"], 32)
            tt(lgt[:, 2, :], lg[:, 0, :], lg[:, 1, :], ALU.max)
            fence()
            for i in range(L):
                m = tt(lgt[:, i, :], lg[:, i, :], lgt[:, 2, :], ALU.subtract)
            m.then_inc(S["lgexp_in"], 1)
            dve.wait_ge(S["lgexp_out"], 1)
            tt(lgt[:, 0, :], lgt[:, 2, :], lgt[:, 3, :], ALU.add)
            fence()
            nc.vector.reciprocal(lgt[:, 1, :], lgt[:, 0, :])
            nc.vector.memset(lbt[:, 0, :], 0.0)
            fence()
            mul(lbt[:, 1, :], lgt[:, 3, :], lgt[:, 1, :])
            dve.wait_ge(S["x_loaded"], 16)
            dve.wait_ge(S["zero_ready"], 2)
            fence()

            def norm_in(l, idx, gname):
                dve.wait_ge(S["rt_ready"], l * 6 + (idx + 1))
                nc.vector.reciprocal(rs[:, :], rt[:, :])
                fence()
                for k in range(KD):
                    m = stt(u[:, k, :], x[:, k, :], pcol(gname, k), rs[:, :], ALU.mult, ALU.mult)
                m.then_inc(S["u_ready"], 1)

            def norm_out(l, idx, gname, step):
                dve.wait_ge(S["rt_ready"], l * 6 + (idx + 1))
                nc.vector.reciprocal(rs[:, :], rt[:, :])
                fence()
                for k in range(KD):
                    stt(ho[:, k, :], ho[:, k, :], pcol(gname, k), rs[:, :], ALU.mult, ALU.mult)
                fence()
                stt(x[:, :, :], ho[:, :, :], step, x[:, :, :], ALU.mult, ALU.add).then_inc(S["x_new"], 1)

            def ffn(l, b, f):
                names = (("ffn1_pre_g", "ffn1_post_g"), ("ffn2_pre_g", "ffn2_post_g"))[f]
                norm_in(l, 4 * f, names[0])
                q = (Q_F1, Q_F2)[f]
                with dve.Fori(0, KF // 2) as i:
                    dve.wait_ge(pair_free[0], l * (NPAIR // 2) + i + (q // 2 + 2))
                    wait_block(dve, l, i * 2 + (b + 1))
                    mul(tiles_at(hff, i * 2, 2), dps[:, 2:4, 0:T], gs[:, :, :]).then_inc(pair_free[1], 1)
                    dve.drain().then_inc(S["h_ready"], 1)
                norm_out(l, 4 * f + 1, names[1], 0.5)

            def token_shift(l, src, k0, nk, strided):
                mu0 = PCOL["rwkv_mu"]
                if strided is None:
                    s, sh, mu = src[:, k0:k0 + nk, :], shift_in[:, k0:k0 + nk, :], prm[:, mu0 + k0:mu0 + k0 + nk]
                else:
                    s = src[:, 0:12, :].rearrange("p (i j) t -> p i j t", i=3)[:, :, bass.ds(strided, 1), :]\
                        .rearrange("p i j t -> p i (j t)")
                    sh = shift_in[:, 0:12, :].rearrange("p (i j) t -> p i j t", i=3)[:, :, bass.ds(strided, 1), :]\
                        .rearrange("p i j t -> p i (j t)")
                    mu = prm[:, mu0:mu0 + 12].rearrange("p (i j) -> p i j", i=3)[:, :, bass.ds(strided, 1)]\
                        .rearrange("p i j -> p (i j)")
                d = dd[:, 0:nk, :]
                ds_, sd_ = (v[:, :, TP:T].rearrange("p i (b t) -> p i b t", b=NB) for v in (d, s))
                tt(d[:, :, 1:TP], s[:, :, 0:TP - 1], s[:, :, 1:TP], ALU.subtract)
                ts(d[:, :, 0:1], s[:, :, 0:1], -1.0, ALU.mult)
                for i in range(nk):
                    tt(ds_[:, i, :, 1:TS], sd_[:, i, :, 0:TS - 1], sd_[:, i, :, 1:TS], ALU.subtract)
                    tt(ds_[:, i, :, 0], sh[:, i, :], sd_[:, i, :, 0], ALU.subtract)
                fence()
                mul(d, d, mu.unsqueeze(2).to_broadcast([P, nk, T]))
                fence()
                return tt(xs[:, 0:nk, :], d, s, ALU.add)

            def halves(kind, a, b):
                for h in range(2):
                    r = slice(CH * h, CH * h + CH)
                    m = mul(E[r, kind, :, r], chunks(a[r, :]), chunks(b[r, :]))
                return m

            def rwkv_pair(l, p):
                n = l * HP + p
                token_shift(l, pa, 0, 3, p).then_inc(S["xs_ready"], 1)
                fence()
                r_, k_, v_ = (xs[:, i, :] for i in range(3))
                a_ = tile_at(lo, p + 4)
                mul(kk0, k_, pcol("rwkv_k_k", p).to_broadcast([P, T])).then_inc(S["kk0_ready"], 1)
                ts(logd, tile_at(lo, p), -EM05, ALU.mult)
                ts(bb, a_, 1.0, ALU.subtract, pcol("rwkv_k_a", p), ALU.mult)
                fence()
                nc.vector.tensor_tensor_scan(cum, seg_a, logd, 0.0, ALU.mult, ALU.add)
                stt(kp, bb, 1.0, k_, ALU.add, ALU.mult)
                fence()
                tt(cumm, cum, logd, ALU.subtract).then_inc(S["cumm_ready"], 1)
                stt(rkr, r_, pcol("rwkv_r_k", p), kp, ALU.mult, ALU.mult).then_inc(S["rkr_ready"], 1)
                dve.wait_ge(S["rk_done"], n + 1)
                mul(rkv, mx[:, 2, 0:T], v_)
                dve.wait_ge(S["norm_ready"], n + 1)
                ts(nrm, nrm, 1e-12, ALU.max)
                fence()
                nc.vector.reciprocal(nrm, nrm)
                fence()
                mul(kksq, kk0, nrm)
                fence()
                mul(bb, kksq, a_)
                dve.wait_ge(S["gam_ready"], n + 1)
                halves(0, kksq, gamm)
                halves(1, r_, gam)
                halves(3, kp, igam)
                fence()
                halves(2, bb, igam).then_inc(S["e_ready"], 1)
                for c in range(NCH):
                    dve.wait_ge(S["abq_done"], n * 5 + (c + 1))
                    mask = mask_p if c < NCH - 1 else mask_s
                    mul(abq[:, c, :, :].rearrange("p (a k) s -> p a (k s)", a=2),
                        mx[:, c % 2, :].rearrange("p (a m) -> p a m", a=2),
                        mask.unsqueeze(1).to_broadcast([P, 2, 2 * P])).then_inc(S["abq_ready"], 1)
                fence()

                def level_part(li):
                    nch = NCH if li <= 2 else NCH - 1
                    return mul(ao[li % 2][:, 0:nch, :], abq[:, 0:nch, 0, :],
                               level[:, li, :].unsqueeze(1).to_broadcast([P, nch, P]))

                level_part(0).then_inc(S["ao_ready"], 1)
                fence()
                identb = ident.unsqueeze(1).to_broadcast([P, NCH, P])
                tt(tinvt, identb, ao[0], ALU.subtract)
                level_part(1).then_inc(S["ao_ready"], 1)
                dve.wait_ge(S["z_done"], n * 6 + 1)
                tt(tinv, identb, chunks(mx01[:, 0:640]), ALU.subtract).then_inc(S["t_ready"], 1)
                for li in range(1, 6):
                    nch = NCH if li <= 2 else NCH - 1
                    nt = NCH if li < 2 else NCH - 1 if li < 5 else 0
                    fence()
                    if li < 5:
                        level_part(li + 1).then_inc(S["ao_ready"], 1)
                    dve.wait_ge(S["pt_done"], n * 5 + li)
                    if nt:
                        tt(tinv[:, 0:nt, :], tinv[:, 0:nt, :],
                           mx23[:, 0:nt * P].rearrange("p (c s) -> p c s", c=nt), ALU.subtract)
                    tt(tinvt[:, 0:nch, :], tinvt[:, 0:nch, :],
                       mx01[:, 0:nch * P].rearrange("p (c s) -> p c s", c=nch), ALU.subtract)\
                        .then_inc(S["t_ready"], 1)
                dve.wait_ge(S["ss_free"], n + 1)
                for c in range(NCH - 1):
                    g = gam[:, c * CH + CH - 1:c * CH + CH]
                    dve.wait_ge(S["p_done"], n * 4 + (c + 1))
                    ts(pn[:, :], mx[:, 0, 0:CH], -1.0, ALU.mult).then_inc(S["pn_ready"], 1)
                    if c:
                        ts(stg[:, :], st[:, c, :], g, ALU.mult)
                    dve.wait_ge(S["u_done"], n * 4 + (c + 1))
                    nc.vector.tensor_copy(uu[:, :], mx[:, 1, 0:CH]).then_inc(S["uc_ready"], 1)
                    fence()
                    dve.wait_ge(S["s_done"], n * 4 + (c + 1))
                    if c:
                        stt(st[:, c + 1, :], mx[:, 3, 0:CH], g, stg[:, :], ALU.mult, ALU.add)\
                            .then_inc(S["s_ready"], 1)
                    else:
                        ts(st[:, 1, :], mx[:, 3, 0:CH], g, ALU.mult).then_inc(S["s_ready"], 1)
                    fence()
                dve.wait_ge(S["y_done"], n + 1)
                for h in range(2):
                    r = slice(CH * h, CH * h + CH)
                    m = nc.vector.tensor_copy(YE[r, 0:NCH - 1, r], mx[r, 2, 0:TP].rearrange("p (c v) -> p c v", v=CH))
                m.then_inc(S["ye_ready"], 1)

                maskb = mask_b.unsqueeze(2).to_broadcast([P, NB, CH])

                def own_stream(src):
                    mul(tmpb, streams(src), maskb)
                    fence()
                    nc.vector.tensor_reduce(ps1[:, :], tmpb.rearrange("p b v -> p v b"), AX.X, ALU.add)
                    fence()

                dve.wait_ge(S["sp_done"], n + 1)
                own_stream(mx[:, 0, :])
                stt(pn[:, :], mx[:, 1, 0:CH], -1.0, ps1[:, :], ALU.mult, ALU.subtract).then_inc(S["spn_ready"], 1)
                dve.wait_ge(S["su_done"], n + 1)
                nc.vector.tensor_copy(uu[:, :], mx[:, 0, 0:CH])
                fence()
                mul(ub, uu[:, :].unsqueeze(1).to_broadcast([P, NB, CH]), maskb)
                mul(vb, vtok[:, NCH - 1, :].unsqueeze(1).to_broadcast([P, NB, CH]), maskb)\
                    .then_inc(S["suc_ready"], 1)
                dve.wait_ge(S["sy_done"], n + 1)
                own_stream(mx[:, 2, :])
                for h in range(2):
                    r = slice(CH * h, CH * h + CH)
                    m = tt(YE[r, NCH - 1, r], mx[r, 3, 0:CH], ps1[r, :], ALU.add)
                m.then_inc(S["ye4_ready"], 1)
                dve.wait_ge(S["sst_done"], n + 1)
                tt(ssn[:, :, :], ss[:, :, :], streams(mx[:, 0, :]), ALU.add)
                fence()
                glast = gam[:, TP:T].rearrange("p (b t) -> p b t", b=NB)[:, :, TS - 1:TS]
                mul(ssn[:, :, :], ssn[:, :, :], glast.to_broadcast([P, NB, CH])).then_inc(S["ssn_ready"], 1)
                dve.wait_ge(S["mean_done"], n + 1)
                stt(cum, mx[:, 2, 0:T], -1.0 / CH, logd, ALU.mult, ALU.add).then_inc(S["dev_ready"], 1)
                dve.wait_ge(S["sd_ready"], n + 1)
                nc.vector.reciprocal(kp, kk0)
                fence()
                mul(cum, cum, kp)
                fence()
                ts(cum, cum, pcol("rwkv_ln_g", p), ALU.mult, pcol("rwkv_ln_b", p), ALU.add)
                fence()
                tt(cum, cum, rkv, ALU.add)
                fence()
                mul(tile_at(oa, p), cum, tile_at(lo, p + 8)).then_inc(S["oa_ready"], 1)
                fence()

            def rglru(l):
                dve.wait_ge(S["pbc_ready"], l + 1)
                dve.wait_ge(S["lru_loaded"], l * 32 + 32)
                xps = xp[:, :, 3 + TP:XPW].rearrange("p k (b n) -> p k b n", b=NB)
                xcs = xc[:, :, TP:T].rearrange("p k (b n) -> p k b n", b=NB)
                nc.vector.memset(xp[:, :, 0:3], 0.0)
                nc.vector.tensor_copy(xp[:, :, 3:3 + TP], pbc[:, 0:4, 0:TP])
                for k in range(4):
                    nc.vector.tensor_copy(xps[:, k, :, 0:3], conv_in[:, k, :, :])
                    nc.vector.tensor_copy(xps[:, k, :, 3:3 + TS],
                                          pbc[:, k, TP:T].rearrange("p (b n) -> p b n", b=NB))
                fence()
                for j in range(4):
                    for k in range(4):
                        w = pcol("lru_conv_w", 4 * j + k)
                        for dst, src in ((xc[:, k, 0:TP], xp[:, k, j:j + TP]), (xcs[:, k, :, :], xps[:, k, :, j:j + TS])):
                            if j == 0:
                                m = ts(dst, src, w, ALU.mult, pcol("lru_conv_b", k), ALU.add)
                            else:
                                m = stt(dst, src, w, dst, ALU.mult, ALU.add)
                    if j < 3:
                        fence()
                m.then_inc(S["xc_ready"], 1)
                dve.wait_ge(S["lru_free"], l + 1)
                nc.vector.tensor_copy(conv_out[:, :, 0, :], xp[:, :, TP:TP + 3])
                for k in range(4):
                    nc.vector.tensor_copy(conv_out[:, k, 1:NB + 1, :], xps[:, k, :, TS:TS + 3])
                ts(spc[:, 3, :], pcol("lru_lam", 0, 4), -1.0, ALU.mult, 0.0, ALU.max)
                fence()
                dve.wait_ge(S["spln_ready"], l + 1)
                tt(spc[:, 3, :], spc[:, 3, :], spc[:, 2, :], ALU.add)
                fence()
                ts(spc[:, 4, :], spc[:, 3, :], -8.0, ALU.mult)
                ts(spc[:, 5, :], spc[:, 3, :], 8.0, ALU.mult).then_inc(S["lam_ready"], 1)
                mul(li, li, xc)
                dve.wait_ge(S["a_ready"], l + 1)
                mul(lb_, la, la)
                fence()
                stt(lb_, lb_, 1.0, lth, ALU.add, ALU.mult).then_inc(S["b2_ready"], 1)
                starts = TP, T, TS
                las, lbs = (v[:, :, TP:T].rearrange("p k (b n) -> p k b n", b=NB)[:, :, :, 0] for v in (la, lb_))
                h0 = lru_out[:, :, 1:NB + 1]
                mul(h0, las, lru_in[:, :, :])
                fence()
                mul(la, la, seg_b.unsqueeze(1).to_broadcast([P, 4, T]))
                dve.wait_ge(S["bs_ready"], l + 1)
                mul(lb_, lth, li)
                fence()
                tt(lbs, lbs, h0, ALU.add)
                fence()
                for k in range(4):
                    nc.vector.tensor_tensor_scan(lr[:, k, :], la[:, k, :], lb_[:, k, :], 0.0, ALU.mult, ALU.add)
                fence()
                nc.vector.tensor_copy(lru_out[:, :, 0:1], lr[:, :, TP - 1:TP])
                nc.vector.tensor_copy(lru_out[:, :, 1:NB + 1],
                                      lr[:, :, TP:T].rearrange("p k (b n) -> p k b n", b=NB)[:, :, :, TS - 1])\
                    .then_inc(S["lru_out_ready"], 1)
                mul(ob, lr, lge).then_inc(S["ob_ready"], 1)
                nc.vector.tensor_copy(lbc[:, 1, :], tile_at(lbt, l))
                fence()
                ts(lbc[:, 0, :], lbc[:, 1, :], -1.0, ALU.mult, 1.0, ALU.add)
                fence()

            def hgrn_head(l, p):
                n = l * 4 + p
                dve.wait_ge(S["hsig_ready"], n + 1)
                mul(hq, sgq, tile_at(pbc, p + 8))
                ts(hf, sgf, lbc[:, 0, :][:, bass.ds(p, 1)], ALU.mult, lbc[:, 1, :][:, bass.ds(p, 1)], ALU.add)
                mul(gzs, sgz, tile_at(pbc, p + 20))
                nc.vector.memset(suf, 1.0)
                nc.vector.memset(att, 0.0)
                fence()
                nc.vector.tensor_copy(pre, hf)
                ts(hk, hf, -1.0, ALU.mult, 1.0, ALU.add).then_inc(S["hq_ready"], 1)

                def keep(mask, bank, small=True):
                    mask = mask.bitcast(U32)
                    nc.vector.copy_predicated(att[:, 0:TP].rearrange("p (c t) -> p c t", c=2),
                                              mask.unsqueeze(1).to_broadcast([P, 2, P]),
                                              mx[:, bank, 0:TP].rearrange("p (c t) -> p c t", c=2))
                    if small:
                        nc.vector.copy_predicated(att[0:CH, TP:T], mask[0:CH, 0:CH], mx[0:CH, bank, TP:T])

                for li in range(7):
                    h = 1 << li
                    e = T if li < 3 else TP

                    def part(v, which):
                        return v[:, 0:e].rearrange("p (n w) -> p n w", w=2 * h)[:, :, which * h:which * h + h]

                    def edge(v, which):
                        last = v[:, 0:e].rearrange("p (n w) -> p n w", w=2 * h)[:, :, which * h + h - 1:which * h + h]
                        return last.to_broadcast([P, e // (2 * h), h])

                    fence()
                    mul(part(qp, 1), part(hq, 1), part(pre, 1))
                    mul(part(ks, 0), part(hk, 0), part(suf, 0)).then_inc(S["qk_ready"], 1)
                    mul(part(suf, 0), part(suf, 0), edge(pre, 1))
                    fence()
                    mul(part(pre, 1), part(pre, 1), edge(pre, 0))
                    if li == 0:
                        wait_apart(dve, "att_done", n * 8 + 1)
                        keep(ident, 0)
                        fence()
                    wait_apart(dve, "att_done", n * 8 + (li + 2))
                    keep(level[:, li, :], (li + 1) % 2, li < 3)
                fence()
                mul(ks, hk, suf).then_inc(S["hkt_ready"], 1)
                mul(qp, hq, pre)
                dve.wait_ge(S["hs_free"], n + 1)
                dve.wait_ge(S["ht_ready"], n * 2 + 1)
                mul(hvb[0:CH, :, :], vt3[0:CH, 2, :].unsqueeze(1).to_broadcast([CH, NB, P]),
                    mask_b[0:CH, :].unsqueeze(2).to_broadcast([CH, NB, P])).then_inc(S["hb_ready"], 1)
                glast = pre[:, TP:T].rearrange("p (b t) -> p b t", b=NB)[:, :, TS - 1:TS]
                dve.wait_ge(S["hs_loaded"], n * 16 + 16)
                mul(hsn[:, :, :], hs[:, :, :], glast.to_broadcast([P, NB, P]))
                dve.wait_ge(S["hst1_done"], n + 1)
                nc.vector.tensor_copy(hst[:, 0, :], mx[:, 2, 0:P])
                fence()
                stt(hst[:, 1, :], hst[:, 0, :], pre[:, TP - 1:TP], mx[:, 2, P:2 * P], ALU.mult, ALU.add)\
                    .then_inc(S["hst1_ready"], 1)
                dve.wait_ge(S["hst_done"], n + 1)
                tt(hsn[:, :, :], hsn[:, :, :], streams(mx01), ALU.add).then_inc(S["hsn_ready"], 1)
                dve.wait_ge(S["osd_ready"], n + 1)
                nc.vector.reciprocal(hrs, hrt)
                fence()
                mul(osb, osb, hrs)
                fence()
                stt(tile_at(oc, p), osb, pcol("hgrn_norm_g", p), gzs, ALU.mult, ALU.mult).then_inc(S["oc_ready"], 1)
                fence()

            with dve.Fori(0, L) as l:
                dve.wait_ge(S["prm_loaded"], l * 32 + 32)
                ffn(l, B_F1, 0)
                norm_in(l, 2, "mix_pre_g")
                dve.wait_ge(S["pa_ready"], l + 1)
                dve.wait_ge(S["shift_loaded"], l * 16 + 16)
                token_shift(l, pa, 12, 2, None).then_inc(S["lora_in_ready"], 1)
                dve.wait_ge(S["shift_free"], l + 1)
                nc.vector.tensor_copy(shift_out[:, :, 0:1], pa[:, :, TP - 1:TP])
                nc.vector.tensor_copy(shift_out[:, :, 1:NB + 1],
                                      pa[:, :, TP:T].rearrange("p k (b n) -> p k b n", b=NB)[:, :, :, TS - 1])\
                    .then_inc(S["shift_out_ready"], 1)
                wait_apart(dve, "lora_ready", l * 3 + 3)
                with dve.Fori(0, HP) as p:
                    rwkv_pair(l, p)
                rglru(l)
                with dve.Fori(0, 4) as p:
                    hgrn_head(l, p)
                dve.wait_ge(S["hs_free"], l * 4 + 5)
                for br in range(3):
                    for s in range(2):
                        for half in range(2):
                            if half:
                                wait_block(dve, l, B_PROJ + 2 * br + s)
                            else:
                                dve.wait_ge(S["proj_half"], l * 6 + (2 * br + s + 1))
                            k = 4 * s + 2 * half
                            dst = merged[:, k:k + 2, :] if br == 0 else xs[:, 0:2, :]
                            mul(dst, dps[:, 2 * half:2 * half + 2, 0:T], gate[:, 8 * br + k:8 * br + k + 2, :])\
                                .then_inc(pair_free[half], 1)
                            if br:
                                fence()
                                m = tt(merged[:, k:k + 2, :], merged[:, k:k + 2, :], xs[:, 0:2, :], ALU.add)
                                fence()
                m.then_inc(S["merged_ready"], 1)
                norm_out(l, 3, "mix_post_g", 1.0)
                ffn(l, B_F2, 1)


def tiles_first(a, n):
    a = a.reshape(a.shape[0], n, P, *a.shape[2:])
    return np.moveaxis(a, 2, 1)


def weight_blocks(w, k_parts, width, l):
    w = w[l].reshape(w.shape[1] // P, P, w.shape[2])
    out = []
    for c in range(0, w.shape[2], width):
        k = 0
        for kt in k_parts:
            part = np.moveaxis(w[k:k + kt, :, c:c + width], 0, 1).reshape(P, -1)
            blk = np.zeros((P, BLK), np.float32)
            blk[:, :part.shape[1]] = part
            out.append(blk)
            k += kt
    return out


def kernel(**inputs):
    import concourse.bacc as _bacc
    from concourse.bass_utils import run_bass_kernel_spmd as _run

    I = {k: np.asarray(v) for k, v in inputs.items()}
    blocks = []
    for l in range(L):
        for f in ("ffn1", "ffn2"):
            g, u_ = (weight_blocks(I[f"{f}_w{c}"], [KD], 256, l) for c in "gu")
            ff = [b for two in zip(g, u_) for b in two] + weight_blocks(I[f"{f}_wd"], [8, 8, 6], 256, l)
            if f == "ffn1":
                blocks += ff
                w = I["w_in"]
                blocks += weight_blocks(w[:, :, 0:1536], [KD], 256, l)
                blocks += weight_blocks(w[:, :, 1536:1792], [KD], P, l)
                blocks += weight_blocks(w[:, :, 1792:], [KD], 256, l)
                for name in "abc":
                    blocks += weight_blocks(I[f"proj_{name}"], [4], 512, l)
                blocks += weight_blocks(I["w_out"], [KD], 256, l)
            else:
                blocks += ff
    arrays = {"wstream": np.stack(blocks)}
    small = np.zeros((L, P, 4, 512), np.float32)
    small[:, 0:64, 0], small[:, 64:128, 0], small[:, :, 1] = I["rwkv_w2"], I["rwkv_a2"], I["rwkv_g2"]
    for i, name in enumerate(("lru_wa", "lru_wx")):
        for g in range(8):
            r = 64 * (g % 2)
            small[:, r:r + 64, 2 + i, 64 * g:64 * g + 64] = I[name][:, g]
    arrays["smallw"] = small
    arrays["params"] = np.concatenate([tiles_first(I[n].reshape(L, w * P), w) for n, w in PARAMS], 2)
    arrays["logits"] = np.moveaxis(I["hgrn_lb_logits"].reshape(L, 4, P), 2, 0)
    arrays["consts"] = constants()[0]
    rows = np.concatenate([I["x_prompt"].reshape(TP, D), I["x_sample"].reshape(T - TP, D)], 0)
    arrays["xT"] = np.moveaxis(rows.T.reshape(KD, P, T), 1, 0)
    arrays["st_shift"] = tiles_first(np.moveaxis(I["state_shift"], 1, 2), 14)
    arrays["st_lru"] = tiles_first(np.moveaxis(I["state_lru"], 1, 2), 4)
    conv = np.moveaxis(I["state_conv"], 3, 1)
    arrays["st_conv"] = tiles_first(conv, 4).reshape(L, P, 4, NB * 3)
    rw = I["state_rwkv"].reshape(L, NB, HP, 2, 64, 64)
    arrays["st_rwkv"] = rw.transpose(0, 2, 3, 5, 1, 4).reshape(L * HP, P, NB, 64)
    arrays["st_hgrn"] = I["state_hgrn"].transpose(0, 2, 3, 1, 4).reshape(L * 4, P, NB, P)
    outs = {"yT": (P, KD, T), "o_shift": (L, P, 14, NB + 1), "o_rwkv": (L * HP, P, NB + 1, 64),
            "o_lru": (L, P, 4, NB + 1), "o_conv": (L, P, 4, (NB + 1) * 3), "o_hgrn": (L * 4, P, NB + 1, P)}

    nc = _bacc.Bacc("TRN2", target_bir_lowering=False, num_devices=1)
    arrays = {k: np.ascontiguousarray(v) for k, v in arrays.items()}
    args = {k: nc.dram_tensor(f"in_{k}", v.shape, F32, kind="ExternalInput").ap() for k, v in arrays.items()}
    args.update({k: nc.dram_tensor(f"out_{k}", s, F32, kind="ExternalOutput").ap() for k, s in outs.items()})
    trunk(nc, **args)
    r = _run(nc, [{f"in_{k}": v for k, v in arrays.items()}], core_ids=[0]).results[0]

    y = np.moveaxis(r["out_yT"], 0, 1).reshape(D, T).T
    shift = np.moveaxis(r["out_o_shift"], 1, 2).reshape(L, 1792, NB + 1).transpose(0, 2, 1)
    rwkv = r["out_o_rwkv"].reshape(L, HP, 2, 64, NB + 1, 64).transpose(0, 4, 1, 2, 5, 3)
    rwkv = rwkv.reshape(L, NB + 1, 8, 64, 64)
    lru = np.moveaxis(r["out_o_lru"], 1, 2).reshape(L, 512, NB + 1).transpose(0, 2, 1)
    conv = np.moveaxis(r["out_o_conv"].reshape(L, P, 4, NB + 1, 3), 1, 2).reshape(L, 512, NB + 1, 3)
    conv = conv.transpose(0, 2, 3, 1)
    hgrn = r["out_o_hgrn"].reshape(L, 4, P, NB + 1, P).transpose(0, 3, 1, 2, 4)
    c = np.ascontiguousarray
    return (c(y[:TP].reshape(1, TP, D)), c(y[TP:].reshape(NB, TS, D)),
            *(c(a[:, :1]) for a in (rwkv, shift, lru, conv, hgrn)),
            *(c(a[:, 1:]) for a in (rwkv, shift, lru, conv, hgrn)))
```

```python
from contextlib import ExitStack

import numpy as np

import concourse.bass as bass
from concourse import mybir

F32 = mybir.dt.float32
F32R = mybir.dt.float32r
U32 = mybir.dt.uint32
ALU = mybir.AluOpType
ACT = mybir.ActivationFunctionType
AX = mybir.AxisListType

P = 128
D = 1024
KD = D // P
L = 2
TP = 256
NB = 8
TS = 8
T = TP + NB * TS
DFF = 2816
KF = DFF // P
CH = 64
NCH = T // CH
HP = 4
BLK = 2048
EPS = 1e-6
GN_EPS = 64e-5
EM05 = float(np.exp(-0.5))

B_F1, B_A, B_B, B_C, B_G0, B_G1, B_PROJ, B_OUT, B_F2, NBLK = 0, 34, 42, 46, 54, 58, 66, 72, 76, 110
NFF = 2 * (B_A - B_F1)
Q_F1, Q_A, Q_B, Q_C, Q_G0, Q_G1, Q_PROJ, Q_OUT, Q_F2, NPAIR = 0, 26, 34, 38, 46, 50, 58, 70, 74, 100

PARAMS = [("ffn1_pre_g", 8), ("ffn1_post_g", 8), ("mix_pre_g", 8), ("mix_post_g", 8), ("ffn2_pre_g", 8),
          ("ffn2_post_g", 8), ("rwkv_mu", 14), ("rwkv_w0", 4), ("rwkv_a0", 4), ("rwkv_k_k", 4), ("rwkv_k_a", 4),
          ("rwkv_r_k", 4), ("rwkv_ln_g", 4), ("rwkv_ln_b", 4), ("lru_conv_w", 16), ("lru_conv_b", 4),
          ("lru_ba", 4), ("lru_bx", 4), ("lru_lam", 4), ("hgrn_norm_g", 4)]
PCOL = {}
_n = 0
for _name, _w in PARAMS:
    PCOL[_name] = _n
    _n += _w
NPARAM = _n


def constants():
    i = np.arange(P)
    s, t = i[:, None], i[None, :]
    head = (s // CH) == (t // CH)
    batch = (s // TS) == (t // TS)
    parts = {
        "ident": s == t,
        "ones": np.ones((P, P)),
        "blk": head,
        "istack": (s % CH) == np.arange(CH)[None, :],
        "mask_p": np.concatenate([head & (s < t), head & (s <= t)], 1),
        "mask_s": np.concatenate([batch & (s < t), batch & (s <= t)], 1),
        "level": np.concatenate([((s // (2 * h)) == (t // (2 * h))) & (s % (2 * h) < h) & (t % (2 * h) >= h)
                                 for h in (1, 2, 4, 8, 16, 32, 64)], 1),
        "mask_b": ((s % CH) // TS) == np.arange(NB)[None, :],
    }
    tok = np.arange(T)
    seg_a = np.where(tok < TP, tok % CH != 0, tok % TS != 0)
    seg_b = np.where(tok < TP, tok != 0, tok % TS != 0)
    parts["seg_a"] = np.broadcast_to(seg_a, (P, T))
    parts["seg_b"] = np.broadcast_to(seg_b, (P, T))
    at, n = {}, 0
    for k, v in parts.items():
        at[k] = (n, v.shape[1])
        n += v.shape[1]
    return np.concatenate([v.astype(np.float32) for v in parts.values()], 1), at


CONST_AT = constants()[1]
NCONST = sum(w for _, w in CONST_AT.values())


def trunk(nc, xT, wstream, smallw, params, logits, consts, st_shift, st_rwkv, st_lru, st_conv, st_hgrn,
          yT, o_shift, o_rwkv, o_lru, o_conv, o_hgrn):
    ctx = ExitStack()
    with ctx:
        def sb(name, *shape):
            return ctx.enter_context(nc.sbuf_tensor(name, [P, *shape], F32))

        def shared(name, *shape, views=()):
            with ExitStack() as before:
                split = [before.enter_context(nc.sbuf_tensor(n, [P, *s], F32R)) for n, s in views]
            return sb(name, *shape), *split

        def sem(name):
            return ctx.enter_context(nc.semaphore(name))

        cst = sb("cst", NCONST)

        def const(name, *shape):
            a, w = CONST_AT[name]
            v = cst[:, a:a + w]
            return v.rearrange("p (a b) -> p a b", a=shape[0]) if shape else v

        ident, ones, blk, istack = const("ident"), const("ones"), const("blk"), const("istack")
        mask_p, mask_s, level = const("mask_p"), const("mask_s"), const("level", 7)
        mask_b, seg_a, seg_b = const("mask_b"), const("seg_a"), const("seg_b")
        x = sb("x", KD, T)
        u = sb("u", KD, T)
        ho, uh = shared("ho", KD, T, views=[("uh", (KD, T))])
        sq, ul = shared("sq", KD, T, views=[("ul", (KD, T))])
        rt = sb("rt", T)
        rs = sb("rs", T)
        raw = [sb(f"raw{i}", BLK) for i in range(2)]
        sw = sb("sw", 4, 512)
        prm_all = sb("prm_all", L, NPARAM)
        prm = sb("prm", NPARAM)
        lg = sb("lg", L, 4)
        lbt = sb("lbt", L, 4)
        lgt = sb("lgt", 4, 4)
        lbc = sb("lbc", 2, 4)
        E = sb("E", 5, NCH, P)
        YE = sb("YE", NCH, P)
        epst = sb("epst", 2)
        tmp, *wlo = shared("tmp", 13 * T, views=[("wlo0", (BLK,)), ("wlo1", (BLK,))])
        pair = tmp[:, 0:6 * T].rearrange("p (a t) -> p a t", a=6)
        zs, btok, ktok = (tmp[:, i * T:(i + 2) * T].rearrange("p (c s) -> p c s", c=NCH) for i in (6, 8, 10))
        vtok = tmp[:, 12 * T:13 * T].rearrange("p (c s) -> p c s", c=NCH)
        st = sb("st", NCH, CH)
        stg = sb("stg", CH)
        pn = sb("pn", CH)
        uu = sb("uu", CH)
        ps1 = sb("ps1", CH)
        gchunk = sb("gchunk", NCH - 1)
        gstream = sb("gstream", NB)
        ss = sb("ss", NB, CH)
        ssn = sb("ssn", NB, CH)
        hs = sb("hs", NB, P)
        hsn = sb("hsn", NB, P)
        shift_in = sb("shift_in", 14, NB)
        shift_out = sb("shift_out", 14, NB + 1)
        lru_in = sb("lru_in", 4, NB)
        lru_out = sb("lru_out", 4, NB + 1)
        conv_in = sb("conv_in", 4, NB, 3)
        conv_out = sb("conv_out", 4, NB + 1, 3)
        spc = sb("spc", 6, 4)

        ov, hfh, hfl, *whi = shared("ov", 64, T, views=[("hfh", (KF, T)), ("hfl", (KF, T)), ("whi0", (BLK,)), ("whi1", (BLK,))])
        gs, h32 = ov[:, 60:62, :], ov[:, 62:64, :]
        gate, pbc, oa, lo = ov[:, 0:24, :], ov[:, 24:48, :], ov[:, 48:52, :], ov[:, 52:64, :]
        ob, oc = pbc[:, 0:4, :], pbc[:, 8:12, :]
        pa = gate[:, 0:14, :]
        logd, cum, cumm, kk0, kp, bb, gam, igam, gamm = (gate[:, 14 + i, :] for i in range(9))
        xs, dd = pair[:, 0:3, :], pair[:, 3:6, :]
        kksq, rkr, nrm = (dd[:, i, :] for i in range(3))
        sqf = sq[:, :, :].rearrange("p a t -> p (a t)")
        hof = ho[:, :, :].rearrange("p a t -> p (a t)")

        def chunks(v):
            return v.rearrange("p (c s) -> p c s", c=NCH)

        abq = sqf.rearrange("p (c k s) -> p c k s", c=NCH, k=4)
        ao = [chunks(hof[:, 640 * i:640 * (i + 1)]) for i in range(2)]
        tinv, tinvt = chunks(hof[:, 1280:1920]), chunks(hof[:, 1920:2560])

        y_, ysq = (zs[:, :, :].rearrange("p c s -> p (c s)")[:, i * T:(i + 1) * T] for i in range(2))
        dev, sd = (ktok[:, :, :].rearrange("p c s -> p (c s)")[:, i * T:(i + 1) * T] for i in range(2))
        rsd = btok[:, :, :].rearrange("p c s -> p (c s)")[:, 0:T]

        def streams(v):
            return v.rearrange("p (b v) -> p b v", b=NB)

        ub = streams(zs[:, :, :].rearrange("p c s -> p (c s)")[:, 0:512])
        vb, tmpb = streams(hof[:, 0:512]), streams(hof[:, 640:1152])
        hq, hf, hk = xs[:, 0, :], xs[:, 1, :], xs[:, 2, :]
        pre, suf, gzs = dd[:, 0, :], dd[:, 1, :], dd[:, 2, :]
        qp, ks, att, sgq, sgf, sgz, osb, osq = (ho[:, i, :] for i in range(8))
        qps = qp, zs[:, :, :].rearrange("p c s -> p (c s)")[:, T:2 * T]
        kss = ks, ktok[:, :, :].rearrange("p c s -> p (c s)")[:, T:2 * T]
        vt3 = sqf[:, 0:384].rearrange("p (c v) -> p c v", c=3)
        kt3 = sqf[:, 384:768].rearrange("p (c v) -> p c v", c=3)
        hvb = streams(sqf[:, 768:1792])
        hst = sqf[:, 1792:2048].rearrange("p (b v) -> p b v", b=2)
        hv = ktok[:, :, :].rearrange("p c s -> p (c s)")[:, 0:T]
        hrt = zs[:, :, :].rearrange("p c s -> p (c s)")[:, 0:T]
        hrs = btok[:, :, :].rearrange("p c s -> p (c s)")[:, 0:T]
        XPW = 3 + TP + NB * (3 + TS)
        xp = pair[:, :, :].rearrange("p a t -> p (a t)")[:, 0:4 * XPW].rearrange("p (k n) -> p k n", k=4)
        xc, lr, li, la = sq[:, 0:4, :], sq[:, 4:8, :], ho[:, 0:4, :], ho[:, 4:8, :]
        lth, lb_, lge = lo[:, 0:4, :], lo[:, 4:8, :], lo[:, 8:12, :]
        merged = pbc[:, 12:20, :]

        dps = ctx.enter_context(nc.psum_tensor("dps", [P, 4, 512], F32))
        mx = ctx.enter_context(nc.psum_tensor("mx", [P, 4, 512], F32))
        mx01 = mx[:, 0:2, :].rearrange("p b n -> p (b n)")
        mx23 = mx[:, 2:4, :].rearrange("p b n -> p (b n)")

        names = """const_loaded lg_loaded x_loaded prm_loaded prm_ready sw_loaded shift_loaded lru_loaded ss_loaded hs_loaded
        block_done proj_half x_new sq_ready hi_ready lo_ready uf_ready uh_ready sum_done rt_ready u_ready h_ready
        lgexp_in lgexp_out zero_ready eps_ready pa_ready pbc_ready lora_in_ready lora_act_ready lora_done lora_ready
        kk0_ready kksq_ready kn_done norm_ready rkr_ready rk_done cumm_ready gam_ready ve_ready
        e_ready abq_done abq_ready tok_done tok_ready ao_ready z_done z_ready pt_done t_ready
        p_done pn_ready u_done uc_ready s_done s_ready y_done ye_ready sp_done spn_ready sy_done su_done
        suc_ready sst_done ye4_ready yt_done yt_ready mean_done dev_ready devsq_ready var_done sd_ready oa_ready
        ss_stored ssn_ready shift_stored shift_out_ready
        xc_ready lg_done lgate_ready spln_ready lam_ready a_ready b2_ready bs_ready ob_ready
        lru_out_ready lru_stored
        hsig_ready hq_ready att_done qk_ready ht_done ht_ready hkt_ready hst1_done hst1_ready
        hb_ready hst_done o_done osq_ready om_done osd_ready oc_ready hs_stored hsn_ready
        merged_ready y_stored shift_free lru_free ss_free hs_free""".split()
        S = {n: sem(n) for n in names}
        w_loaded = [sem("w_loaded0"), sem("w_loaded1")]
        pair_free = [sem("pair_free0"), sem("pair_free1")]

        def pcol(name, i, n=1):
            a = PCOL[name]
            return prm[:, a + i:a + i + n] if isinstance(i, int) else prm[:, bass.ds(i + a, n)]

        def tiles_at(t, i, n):
            return t[:, i:i + n, :] if isinstance(i, int) else t[:, bass.ds(i, n), :]

        def tile_at(t, i):
            return t[:, i, :] if isinstance(i, int) else t[:, bass.ds(i, 1), :].rearrange("p a t -> p (a t)")

        def wait_block(eng, l, j):
            eng.wait_ge(S["block_done"], l * NBLK + (j + 3))

        def wait_apart(eng, name, value):
            value = eng.to_reg(value)
            eng.wait_ge(S["const_loaded"], 16)
            eng.wait_ge(S[name], value)

        block = ctx.enter_context(nc.Block())

        @block.sync
        def _(sp):
            sp.dma_start(x[:, :, :], xT).then_inc(S["x_loaded"], 16)
            sp.dma_start(cst[:, :], consts).then_inc(S["const_loaded"], 16)

            def load(l, i, b, s):
                sp.dma_start(raw[s][:, :], wstream[bass.ds(l * NBLK + i * 2 + (b + s), 1), :, :]
                             .rearrange("a p n -> (a p) n")).then_inc(w_loaded[s], 16)

            with sp.Fori(0, L) as l:
                with sp.Fori(0, B_A // 2 + 1) as i:
                    for s in range(2):
                        sp.wait_ge(S["lo_ready"], l * NFF + i * 2 + (s + 1))
                        load(l, i, 0, s)
                with sp.Fori(0, (B_F2 - B_A) // 2) as i:
                    for s in range(2):
                        sp.wait_ge(S["block_done"], l * NBLK + i * 2 + (B_A + 2 + s + 1))
                        load(l, i, B_A + 2, s)
                with sp.Fori(0, B_A // 2 - 1) as i:
                    for s in range(2):
                        sp.wait_ge(S["lo_ready"], l * NFF + i * 2 + (B_A + 2 + s + 1))
                        load(l, i, B_F2 + 2, s)
            sp.wait_ge(S["x_new"], (3 * L + 1) * 4)
            sp.dma_start(yT, x[:, :, :]).then_inc(S["y_stored"], 16)
            sp.wait_ge(S["y_stored"], 16)

        @block.gpsimd
        def _(pool):
            pool.dma_start(prm_all[:, :, :], params.rearrange("l p n -> p l n")).then_inc(S["prm_loaded"], 16)
            pool.dma_start(lg[:, :, :], logits).then_inc(S["lg_loaded"], 16)
            for free in ("shift_free", "lru_free", "ss_free", "hs_free"):
                pool.sem_inc(S[free], 1)

            def lay(t, l):
                return t[bass.ds(l, 1)]

            with pool.Fori(0, L) as l:
                wait_apart(pool, "x_new", l * 12 + 4)
                pool.dma_start(sw[:, :, :], lay(smallw, l).rearrange("a p k n -> (a p) k n"))\
                    .then_inc(S["sw_loaded"], 16)
                pool.dma_start(shift_in[:, :, :], lay(st_shift, l).rearrange("a p k n -> (a p) k n"))\
                    .then_inc(S["shift_loaded"], 16)
                pool.dma_start(lru_in[:, :, :], lay(st_lru, l).rearrange("a p k n -> (a p) k n"))\
                    .then_inc(S["lru_loaded"], 16)
                pool.dma_start(conv_in[:, :, :, :].rearrange("p k b n -> p k (b n)"),
                               lay(st_conv, l).rearrange("a p k n -> (a p) k n")).then_inc(S["lru_loaded"], 16)
                wait_apart(pool, "shift_out_ready", l + 1)
                pool.dma_start(lay(o_shift, l).rearrange("a p k n -> (a p) k n"), shift_out[:, :, :])\
                    .then_inc(S["shift_stored"], 16)
                pool.wait_ge(S["shift_stored"], l * 16 + 16)
                pool.sem_inc(S["shift_free"], 1)
                with pool.Fori(0, HP) as p:
                    n = l * HP + p
                    wait_apart(pool, "oa_ready", n + 1)
                    pool.dma_start(ss[:, :, :], st_rwkv[bass.ds(n, 1)].rearrange("a p b v -> (a p) b v"))\
                        .then_inc(S["ss_loaded"], 16)
                    wait_apart(pool, "ssn_ready", n + 1)
                    pool.dma_start(o_rwkv[bass.ds(n, 1), :, 0:1, :].rearrange("a p b v -> (a p) (b v)"), st[:, 4, :])\
                        .then_inc(S["ss_stored"], 16)
                    pool.dma_start(o_rwkv[bass.ds(n, 1), :, 1:NB + 1, :].rearrange("a p b v -> (a p) b v"),
                                   ssn[:, :, :]).then_inc(S["ss_stored"], 16)
                    pool.wait_ge(S["ss_stored"], n * 32 + 32)
                    pool.sem_inc(S["ss_free"], 1)
                wait_apart(pool, "lru_out_ready", l + 1)
                pool.dma_start(lay(o_lru, l).rearrange("a p k n -> (a p) k n"), lru_out[:, :, :])\
                    .then_inc(S["lru_stored"], 16)
                pool.dma_start(lay(o_conv, l).rearrange("a p k n -> (a p) k n"),
                               conv_out[:, :, :, :].rearrange("p k b n -> p k (b n)")).then_inc(S["lru_stored"], 16)
                pool.wait_ge(S["lru_stored"], l * 32 + 32)
                pool.sem_inc(S["lru_free"], 1)
                with pool.Fori(0, 4) as p:
                    n = l * 4 + p
                    wait_apart(pool, "oc_ready", n + 1)
                    pool.dma_start(hs[:, :, :], st_hgrn[bass.ds(n, 1)].rearrange("a p b v -> (a p) b v"))\
                        .then_inc(S["hs_loaded"], 16)
                    wait_apart(pool, "hsn_ready", n + 1)
                    pool.dma_start(o_hgrn[bass.ds(n, 1), :, 0:1, :].rearrange("a p b v -> (a p) (b v)"), hst[:, 1, :])\
                        .then_inc(S["hs_stored"], 16)
                    pool.dma_start(o_hgrn[bass.ds(n, 1), :, 1:NB + 1, :].rearrange("a p b v -> (a p) b v"),
                                   hsn[:, :, :]).then_inc(S["hs_stored"], 16)
                    pool.wait_ge(S["hs_stored"], n * 32 + 32)
                    pool.sem_inc(S["hs_free"], 1)
            pool.wait_ge(S["shift_stored"], 16 * L)
            pool.wait_ge(S["lru_stored"], 32 * L)
            pool.wait_ge(S["ss_stored"], 32 * HP * L)
            pool.wait_ge(S["hs_stored"], 32 * 4 * L)

        @block.tensor
        def _(pe):
            pe.sem_inc(S["block_done"], 2)
            pe.wait_ge(S["const_loaded"], 16)

            def block_in(l, half, s):
                pe.wait_ge(w_loaded[s], (l * (NBLK // 2) + half) * 16 + 16)

            def pair_wait(l, qhalf, s):
                pe.wait_ge(pair_free[s], l * (NPAIR // 2) + qhalf + 1)

            def tiles(s, kt, width, src, half, cols=(0, 1), col0=0, fresh=None):
                w = raw[s][:, 0:kt * width].rearrange("p (k n) -> p k n", k=kt)
                for c in cols:
                    for k in range(kt):
                        if fresh and c == 0 and k % 2 == 0:
                            u_wait(*fresh, k)
                        m = pe.matmul(dps[:, 2 * half + c, 0:T], w[:, k, (col0 + c) * P:(col0 + c + 1) * P],
                                      src[:, k, :], start=k == 0, stop=k == kt - 1, skip_group_check=True)
                return m

            def norm_sum(l, idx, turns=range(4)):
                for j in turns:
                    pe.wait_ge(S["sq_ready"], l * 24 + (4 * idx + j + 1))
                    for k in (2 * j, 2 * j + 1):
                        m = pe.matmul(mx[:, 3, 0:T], ones, sq[:, k, :], start=k == 0, stop=k == KD - 1,
                                      skip_group_check=True)
                    if j == 3:
                        m.then_inc(S["sum_done"], 1)

            def u_wait(l, n, k):
                pe.wait_ge(S["u_ready"], l * 12 + (4 * n + k // 2 + 1))

            def dense(l, b, q, turns, n_in=None):
                with pe.Fori(0, turns) as i:
                    for s in range(2):
                        block_in(l, i + b // 2, s)
                        pair_wait(l, i + q // 2, s)
                        tiles(s, KD, 256, u, s, fresh=None if n_in is None or s else (l, n_in))\
                            .then_inc(S["block_done"], 1)

            def split_tiles(s, kt, hi, lo_, half, first=True, last=True, k0=0, fresh=None):
                wh, wl = (v[s][:, 0:kt * 256].rearrange("p (k n) -> p k n", k=kt) for v in (whi, wlo))
                for c in range(2):
                    for k in range(kt):
                        if fresh and c == 0 and k % 2 == 0:
                            u_wait(*fresh, k)
                        for i, (w, v) in enumerate(((wh, hi), (wh, lo_), (wl, hi))):
                            m = pe.matmul(dps[:, 2 * half + c, 0:T], w[:, k, c * P:(c + 1) * P], v[:, k0 + k, :],
                                          start=first and k == 0 and i == 0, stop=last and k == kt - 1 and i == 2,
                                          skip_group_check=True)
                return m

            def ffn(l, b, q, f):
                def split_in(i, j):
                    pe.wait_ge(S["lo_ready"], l * NFF + i * 2 + (B_A * f + j + 3))

                norm_sum(l, 4 * f)
                with pe.Fori(0, KF // 2) as i:
                    for s in range(2):
                        split_in(i, s)
                        pair_wait(l, i + q // 2, s)
                        split_tiles(s, KD, uh[:, :, :], ul[:, :, :], s, fresh=None if s else (l, 2 * f))\
                            .then_inc(S["block_done"], 1)
                for j in range(12):
                    half, part = j // 3, j % 3
                    pe.wait_ge(S["lo_ready"], l * NFF + (B_A * f + KF + j + 3))
                    if part == 0:
                        pair_wait(l, (q + KF + half) // 2, half % 2)
                    pe.wait_ge(S["h_ready"], l * 22 + (11 * f + 1 + (4, 8, 11)[part]))
                    split_tiles(j % 2, 8 if part < 2 else 6, hfh, hfl, half % 2, first=part == 0, last=part == 2,
                                k0=8 * part).then_inc(S["block_done"], 1)
                    if j in (4, 7, 10):
                        norm_sum(l, 4 * f + 1, (j // 3 - 1,))
                norm_sum(l, 4 * f + 1, (3,))

            def key_sums(l, p):
                n = l * HP + p
                pe.wait_ge(S["kksq_ready"], n + 1)
                pe.matmul(mx[:, 3, 0:T], blk, kksq, start=True, stop=True).then_inc(S["kn_done"], 1)
                pe.wait_ge(S["rkr_ready"], n + 1)
                pe.matmul(mx[:, 1, 0:T], blk, rkr, start=True, stop=True).then_inc(S["rk_done"], 1)

            def attention(l, p, chunks_):
                n = l * HP + p
                for c in chunks_:
                    if c >= 2:
                        pe.wait_ge(S["abq_ready"], n * 5 + (c - 1))
                    pe.matmul(mx[:, c % 2, 0:256], E[:, 2, c, :], E[:, 0:2, c, :], start=True, stop=True,
                              skip_group_check=True)
                    pe.matmul(mx[:, c % 2, 256:512], E[:, 3, c, :], E[:, 0:2, c, :], start=False, stop=True,
                              skip_group_check=True).then_inc(S["abq_done"], 1)

            def rwkv_pair(l, p, more):
                n = l * HP + p

                def filler(f):
                    s, c = f // 2, f % 2
                    if c == 0:
                        block_in(l, p + B_C // 2, s)
                        pair_wait(l, p + Q_C // 2, s)
                    m = tiles(s, KD, 256, u, s, cols=(c,))
                    if c == 1:
                        m.then_inc(S["block_done"], 1)

                pe.wait_ge(S["oa_ready"], n + 1)
                for c in range(NCH):
                    m = pe.transpose(mx23[:, c * P:(c + 1) * P], E[:, 2, c, :], ident)
                m.then_inc(S["tok_done"], 1)
                pe.wait_ge(S["abq_ready"], n * 5 + 5)
                for c in range(NCH):
                    m = pe.transpose(mx01[:, c * P:(c + 1) * P], E[:, 3, c, :], ident)
                m.then_inc(S["tok_done"], 1)
                pe.wait_ge(S["ve_ready"], n + 1)
                pe.wait_ge(S["tok_ready"], n * 3 + 1)
                for c in range(NCH):
                    m = pe.matmul(mx[:, 2, c * CH:(c + 1) * CH], E[:, 4, c, :], istack, start=True, stop=True)
                m.then_inc(S["tok_done"], 1)
                pe.wait_ge(S["ao_ready"], n * 6 + 1)
                pe.wait_ge(S["tok_ready"], n * 3 + 2)
                for c in range(NCH):
                    m = pe.transpose(mx01[:, c * P:(c + 1) * P], ao[0][:, c, :], ident)
                m.then_inc(S["z_done"], 1)
                filler(0)
                pe.wait_ge(S["tok_ready"], n * 3 + 3)
                for li in range(1, 6):
                    nch = NCH if li <= 2 else NCH - 1
                    nt = NCH if li < 2 else NCH - 1 if li < 5 else 0
                    pe.wait_ge(S["ao_ready"], n * 6 + (li + 1))
                    pe.wait_ge(S["t_ready"], n * 6 + li)
                    if li == 4 and more:
                        key_sums(l, p + 1)
                    for c in range(nch):
                        m = pe.matmul(mx01[:, c * P:(c + 1) * P], ao[li % 2][:, c, :], tinv[:, c, :],
                                      start=True, stop=True)
                    m.then_inc(S["z_done"], 1)
                    if li == 1:
                        filler(1)
                    pe.wait_ge(S["z_ready"], n * 5 + li)
                    for c in range(nt):
                        pe.matmul(mx23[:, c * P:(c + 1) * P], tinvt[:, c, :], zs[:, c, :], start=True, stop=True)
                    for c in range(nch):
                        m = pe.matmul(mx01[:, c * P:(c + 1) * P], zs[:, c, :], tinvt[:, c, :], start=True, stop=True)
                    m.then_inc(S["pt_done"], 1)
                pe.wait_ge(S["t_ready"], n * 6 + 6)
                aE, rE = E[:, 0, :, :], E[:, 1, :, :]
                for c in range(NCH - 1):
                    pe.matmul(mx[:, 0, 0:CH], abq[:, c, 2, :], vtok[:, c, :], start=True, stop=c == 0)\
                        .then_inc(S["p_done"], 1) if c == 0 else \
                        pe.matmul(mx[:, 0, 0:CH], abq[:, c, 2, :], vtok[:, c, :], start=True, stop=False)
                    if c > 0:
                        pe.wait_ge(S["s_ready"], n * 4 + c)
                        pe.matmul(mx[:, 0, 0:CH], aE[:, c, :], st[:, c, :], start=False, stop=True)\
                            .then_inc(S["p_done"], 1)
                    pe.wait_ge(S["pn_ready"], n * 4 + (c + 1))
                    pe.matmul(mx[:, 1, 0:CH], tinvt[:, c, :], pn[:, :], start=True, stop=True).then_inc(S["u_done"], 1)
                    pe.wait_ge(S["uc_ready"], n * 4 + (c + 1))
                    pe.matmul(mx[:, 3, 0:CH], btok[:, c, :], uu[:, :], start=True, stop=False)
                    pe.matmul(mx[:, 3, 0:CH], ktok[:, c, :], vtok[:, c, :], start=False, stop=True)\
                        .then_inc(S["s_done"], 1)
                    yc = mx[:, 2, c * CH:(c + 1) * CH]
                    if c > 0:
                        pe.matmul(yc, rE[:, c, :], st[:, c, :], start=True, stop=False)
                    pe.matmul(yc, abq[:, c, 1, :], uu[:, :], start=c == 0, stop=False)
                    m = pe.matmul(yc, abq[:, c, 3, :], vtok[:, c, :], start=False, stop=True)
                m.then_inc(S["y_done"], 1)
                c = NCH - 1
                ssf = ss[:, :, :].rearrange("p b v -> p (b v)")
                pe.wait_ge(S["ss_loaded"], n * 16 + 16)
                pe.matmul(mx[:, 0, :], aE[:, c, :], ssf, start=True, stop=True)
                pe.matmul(mx[:, 1, 0:CH], abq[:, c, 2, :], vtok[:, c, :], start=True, stop=True)\
                    .then_inc(S["sp_done"], 1)
                pe.wait_ge(S["ye_ready"], n + 1)
                pe.matmul(mx[:, 2, :], rE[:, c, :], ssf, start=True, stop=True)
                pe.wait_ge(S["spn_ready"], n + 1)
                pe.matmul(mx[:, 0, 0:CH], tinvt[:, c, :], pn[:, :], start=True, stop=True).then_inc(S["su_done"], 1)
                pe.wait_ge(S["suc_ready"], n + 1)
                pe.matmul(mx[:, 3, 0:CH], abq[:, c, 1, :], uu[:, :], start=True, stop=False)
                pe.matmul(mx[:, 3, 0:CH], abq[:, c, 3, :], vtok[:, c, :], start=False, stop=True)\
                    .then_inc(S["sy_done"], 1)
                pe.matmul(mx[:, 0, :], btok[:, c, :], ub.rearrange("p b v -> p (b v)"), start=True, stop=False)
                pe.matmul(mx[:, 0, :], ktok[:, c, :], vb.rearrange("p b v -> p (b v)"), start=False, stop=True)\
                    .then_inc(S["sst_done"], 1)
                pe.wait_ge(S["ye4_ready"], n + 1)
                for c in range(NCH):
                    m = pe.matmul(mx[:, 3, c * CH:(c + 1) * CH], YE[:, c, :], istack, start=True, stop=True)
                m.then_inc(S["yt_done"], 1)
                pe.wait_ge(S["yt_ready"], n + 1)
                pe.matmul(mx[:, 2, 0:T], blk, y_, start=True, stop=True).then_inc(S["mean_done"], 1)
                if more:
                    pe.wait_ge(S["ssn_ready"], n + 1)
                    pe.wait_ge(S["e_ready"], n + 2)
                    attention(l, p + 1, (0, 1))
                pe.wait_ge(S["devsq_ready"], n + 1)
                pe.matmul(mx[:, 3, 0:T], blk, ysq, start=True, stop=True).then_inc(S["var_done"], 1)
                filler(2)
                if more:
                    attention(l, p + 1, (2, 3))
                filler(3)
                if more:
                    attention(l, p + 1, (4,))

            def hgrn_head(l, p):
                n = l * 4 + p
                SPAN = [(0, P), (P, 2 * P), (2 * P, T)]

                def filler(f):
                    s, c = f // 2, f % 2
                    if c == 0:
                        block_in(l, p + B_G1 // 2, s)
                        pair_wait(l, p + Q_G1 // 2, s)
                    m = tiles(s, KD, 256, u, s, cols=(c,))
                    if c == 1:
                        m.then_inc(S["block_done"], 1)

                pe.wait_ge(S["oc_ready"], n + 1)
                pe.wait_ge(S["hsig_ready"], n + 1)
                for c, (a, b) in enumerate(SPAN):
                    m = pe.transpose(mx[0:b - a, 2, c * P:(c + 1) * P], hv[:, a:b], ident)
                m.then_inc(S["ht_done"], 1)
                filler(0)
                pe.wait_ge(S["hq_ready"], n + 1)
                for a, b in SPAN:
                    m = pe.matmul(mx[0:b - a, 0, a:b], hk[:, a:b], hq[:, a:b], start=True, stop=True)
                m.then_inc(S["att_done"], 1)
                for li in range(7):
                    pe.wait_ge(S["qk_ready"], n * 7 + (li + 1))
                    for a, b in SPAN if li < 3 else SPAN[:2]:
                        m = pe.matmul(mx[0:b - a, (li + 1) % 2, a:b], kss[li % 2][:, a:b], qps[li % 2][:, a:b], start=True, stop=True)
                    m.then_inc(S["att_done"], 1)
                pe.wait_ge(S["hkt_ready"], n + 1)
                for c, (a, b) in enumerate(SPAN):
                    m = pe.transpose(mx[0:b - a, 3, c * P:(c + 1) * P], kss[1][:, a:b], ident)
                m.then_inc(S["ht_done"], 1)
                filler(1)
                pe.wait_ge(S["ht_ready"], n * 2 + 2)
                pe.matmul(mx[:, 2, 0:P], kt3[:, 0, :], vt3[:, 0, :], start=True, stop=True)
                pe.matmul(mx[:, 2, P:2 * P], kt3[:, 1, :], vt3[:, 1, :], start=True, stop=True)\
                    .then_inc(S["hst1_done"], 1)
                pe.wait_ge(S["hb_ready"], n + 1)
                for j in range(2):
                    m = pe.matmul(mx[:, j, :], kt3[0:CH, 2, :], hvb[0:CH, 4 * j:4 * j + 4, :], start=True, stop=True)
                m.then_inc(S["hst_done"], 1)
                pe.wait_ge(S["hst1_ready"], n + 1)
                pe.wait_ge(S["hs_loaded"], n * 16 + 16)
                pe.matmul(mx[:, 3, 0:P], vt3[:, 0, :], att[:, 0:P], start=True, stop=True)
                pe.matmul(mx[:, 3, P:2 * P], vt3[:, 1, :], att[:, P:2 * P], start=True, stop=False)
                pe.matmul(mx[:, 3, P:2 * P], hst[:, 0, :], qps[1][:, P:2 * P], start=False, stop=True)
                pe.matmul(mx[:, 3, 2 * P:T], vt3[0:CH, 2, :], att[0:CH, 2 * P:T], start=True, stop=False)
                for b in range(NB):
                    t0 = TP + b * TS
                    m = pe.matmul(mx[:, 3, t0:t0 + TS], hs[:, b, :], qps[1][:, t0:t0 + TS], start=False, stop=b == NB - 1)
                m.then_inc(S["o_done"], 1)
                pe.wait_ge(S["osq_ready"], n + 1)
                pe.matmul(mx[:, 2, 0:T], ones, osq, start=True, stop=True).then_inc(S["om_done"], 1)
                filler(2)
                filler(3)

            with pe.Fori(0, L) as l:
                ffn(l, B_F1, Q_F1, 0)
                norm_sum(l, 2)
                dense(l, B_A, Q_A, 3, n_in=1)
                for s in range(2):
                    block_in(l, B_A // 2 + 3, s)
                    pair_wait(l, Q_A // 2 + 3, s)
                    tiles(s, KD, P, u, s, cols=(0,)).then_inc(S["block_done"], 1)
                dense(l, B_B, Q_B, 1)
                pe.wait_ge(S["sw_loaded"], l * 16 + 16)
                pe.wait_ge(S["lora_act_ready"], l + 1)
                for kind in range(3):
                    if kind:
                        pe.wait_ge(S["lora_ready"], l * 3 + kind)
                    a, b, which = ((0, CH, 0), (CH, P, 0), (0, P, 1))[kind]
                    src = kp if kind == 2 else bb
                    for j in range(4):
                        m = pe.matmul(mx[:, j, 0:T], sw[a:b, which, j * P:(j + 1) * P], src[a:b, :], start=True, stop=True)
                    m.then_inc(S["lora_done"], 1)
                dense(l, B_B + 2, Q_B + 2, 1)
                key_sums(l, 0)
                pe.wait_ge(S["e_ready"], l * HP + 1)
                attention(l, 0, range(NCH))
                with pe.Fori(0, HP - 1) as p:
                    rwkv_pair(l, p, True)
                rwkv_pair(l, HP - 1, False)
                dense(l, B_G0, Q_G0, 1)
                pe.wait_ge(S["xc_ready"], l + 1)
                for kind in range(2):
                    if kind:
                        pe.wait_ge(S["lgate_ready"], l * 2 + 1)
                    for j in range(4):
                        m = pe.matmul(mx[:, j, 0:T], sw[:, 2 + kind, j * P:(j + 1) * P], xc[:, j, :], start=True, stop=True)
                    m.then_inc(S["lg_done"], 1)
                dense(l, B_G0 + 2, Q_G0 + 2, 1)
                with pe.Fori(0, 4) as p:
                    hgrn_head(l, p)
                pe.wait_ge(S["ob_ready"], l + 1)
                pe.wait_ge(S["oc_ready"], l * 4 + 5)
                for br, src in enumerate((oa, ob, oc)):
                    for s in range(2):
                        block_in(l, B_PROJ // 2 + br, s)
                        for half in range(2):
                            pair_wait(l, (Q_PROJ + 4 * br + 2 * s) // 2, half)
                            m = tiles(s, 4, 512, src, half, col0=2 * half)
                            m.then_inc(S["block_done"] if half else S["proj_half"], 1)
                wait_apart(pe, "merged_ready", l + 1)
                for j in range(4):
                    block_in(l, (B_OUT + j) // 2, j % 2)
                    pair_wait(l, (Q_OUT + j) // 2, j % 2)
                    tiles(j % 2, KD, 256, merged, j % 2).then_inc(S["block_done"], 1)
                    if j:
                        norm_sum(l, 3, (j - 1,))
                norm_sum(l, 3, (3,))
                ffn(l, B_F2, Q_F2, 1)

        @block.scalar
        def _(act):
            def fn(out, in_, f, **kw):
                return nc.scalar.activation(out, in_, f, **kw)

            act.wait_ge(S["const_loaded"], 16)
            act.wait_ge(S["zero_ready"], 2)
            act.wait_ge(S["eps_ready"], 2)
            act.wait_ge(S["x_loaded"], 16)
            act.wait_ge(S["lgexp_in"], 1)
            fn(lgt[:, 2:4, :], lgt[:, 0:2, :], ACT.Exp).then_inc(S["lgexp_out"], 1)

            def root(l, idx):
                act.wait_ge(S["sum_done"], l * 6 + (idx + 1))
                fn(rt[:, :], mx[:, 3, 0:T], ACT.Sqrt, scale=1.0 / D, bias=epst[:, 0:1]).then_inc(S["rt_ready"], 1)

            def norm(l, idx):
                for j in range(4):
                    act.wait_ge(S["x_new"], l * 12 + (4 * (idx // 2) + j + 1))
                    fn(sq[:, 2 * j:2 * j + 2, :], x[:, 2 * j:2 * j + 2, :], ACT.Square).then_inc(S["sq_ready"], 1)
                root(l, idx)

            def read_squared(l, j, s, k):
                wait_block(act, l, j)
                src = dps[:, 2 * s:2 * s + 2, 0:T]
                fn(sq[:, k:k + 2, :], src, ACT.Square).then_inc(S["sq_ready"], 1)
                fn(ho[:, k:k + 2, :], src, ACT.Copy).then_inc(pair_free[s], 1)

            def split_hi(l, i, j, s, f):
                act.wait_ge(w_loaded[s], (l * (NBLK // 2) + i + ((0, B_F2)[f] + j) // 2) * 16 + 16)
                wait_block(act, l, i * 2 + ((0, B_F2)[f] + j - 2))
                fn(whi[s][:, :], raw[s][:, :], ACT.Copy).then_inc(S["hi_ready"], 1)

            def read_pair(l, j, s, dst, f, n=2):
                wait_block(act, l, j)
                return fn(dst, dps[:, 2 * s:2 * s + n, 0:T], f)

            def ffn(l, b, f):
                for s in range(2):
                    split_hi(l, 0, s, s, f)
                norm(l, 4 * f)
                for j in range(4):
                    act.wait_ge(S["uf_ready"], l * 8 + (4 * f + j + 1))
                    fn(uh[:, 2 * j:2 * j + 2, :], u[:, 2 * j:2 * j + 2, :], ACT.Copy)\
                        .then_inc(S["uh_ready"], 1)
                with act.Fori(0, KF // 2) as i:
                    act.wait_ge(S["h_ready"], l * 22 + i + (11 * f + 1))
                    read_pair(l, i * 2 + b, 0, gs[:, :, :], ACT.Silu).then_inc(pair_free[0], 1)
                    for s in range(2):
                        split_hi(l, i, 2 + s, s, f)
                for j in range(12):
                    if j % 3 == 2:
                        read_squared(l, b + KF + j, j // 3 % 2, j // 3 * 2)
                    if j < 10:
                        split_hi(l, 0, KF + j + 2, j % 2, f)
                root(l, 4 * f + 1)

            def key_square(n):
                act.wait_ge(S["kk0_ready"], n + 1)
                fn(kksq, kk0, ACT.Square).then_inc(S["kksq_ready"], 1)

            def key_norm(n):
                act.wait_ge(S["kn_done"], n + 1)
                fn(nrm, mx[:, 3, 0:T], ACT.Sqrt).then_inc(S["norm_ready"], 1)

            def decays(n):
                act.wait_ge(S["cumm_ready"], n + 1)
                fn(gam, cum, ACT.Exp)
                fn(igam, cum, ACT.Exp, scale=-1.0)
                fn(gamm, cumm, ACT.Exp).then_inc(S["gam_ready"], 1)
                for h in range(2):
                    r = slice(CH * h, CH * h + CH)
                    m = fn(E[r, 4, :, r], chunks(xs[r, 2, :]), ACT.Copy)
                m.then_inc(S["ve_ready"], 1)

            def rwkv_pair(l, p, more):
                n = l * HP + p
                act.wait_ge(S["tok_done"], n * 3 + 1)
                fn(btok[:, :, :], chunks(mx23[:, 0:640]), ACT.Copy).then_inc(S["tok_ready"], 1)
                act.wait_ge(S["tok_done"], n * 3 + 2)
                fn(ktok[:, :, :], chunks(mx01[:, 0:640]), ACT.Copy).then_inc(S["tok_ready"], 1)
                act.wait_ge(S["tok_done"], n * 3 + 3)
                fn(vtok[:, :, :], chunks(mx[:, 2, 0:T]), ACT.Copy).then_inc(S["tok_ready"], 1)
                for li in range(1, 6):
                    nch = NCH if li <= 2 else NCH - 1
                    act.wait_ge(S["z_done"], n * 6 + (li + 1))
                    fn(zs[:, 0:nch, :], mx01[:, 0:nch * P].rearrange("p (c s) -> p c s", c=nch), ACT.Copy)\
                        .then_inc(S["z_ready"], 1)
                    if li == 2:
                        read_pair(l, p * 2 + B_C, 0, tiles_at(pbc, p * 4 + 8, 2), ACT.Copy).then_inc(pair_free[0], 1)
                    if li == 3 and more:
                        key_square(n + 1)
                    if li == 4 and more:
                        key_norm(n + 1)
                if more:
                    decays(n + 1)
                act.wait_ge(S["yt_done"], n + 1)
                fn(y_, mx[:, 3, 0:T], ACT.Copy).then_inc(S["yt_ready"], 1)
                act.wait_ge(S["dev_ready"], n + 1)
                fn(ysq, dev, ACT.Square).then_inc(S["devsq_ready"], 1)
                act.wait_ge(S["var_done"], n + 1)
                fn(sd, mx[:, 3, 0:T], ACT.Sqrt, scale=1.0 / CH, bias=epst[:, 1:2]).then_inc(S["sd_ready"], 1)
                read_pair(l, p * 2 + (B_C + 1), 1, tiles_at(pbc, p * 4 + 10, 2), ACT.Copy).then_inc(pair_free[1], 1)

            def head_functions(l, p):
                for dst, t in ((sgq, 8), (sgf, 12), (sgz, 20)):
                    fn(dst, tile_at(pbc, p + t), ACT.Sigmoid)
                fn(hv, tile_at(pbc, p + 16), ACT.Copy).then_inc(S["hsig_ready"], 1)

            def hgrn_head(l, p, more):
                n = l * 4 + p
                act.wait_ge(S["ht_done"], n * 2 + 1)
                fn(vt3[:, 0:2, :], mx[:, 2, 0:2 * P].rearrange("p (c v) -> p c v", c=2), ACT.Copy)
                fn(vt3[0:CH, 2, :], mx[0:CH, 2, 2 * P:3 * P], ACT.Copy).then_inc(S["ht_ready"], 1)
                if more:
                    act.wait_ge(S["hq_ready"], n + 1)
                    head_functions(l, p + 1)
                act.wait_ge(S["ht_done"], n * 2 + 2)
                fn(kt3[:, 0:2, :], mx[:, 3, 0:2 * P].rearrange("p (c v) -> p c v", c=2), ACT.Copy)
                fn(kt3[0:CH, 2, :], mx[0:CH, 3, 2 * P:3 * P], ACT.Copy).then_inc(S["ht_ready"], 1)
                act.wait_ge(S["o_done"], n + 1)
                fn(osb, mx[:, 3, 0:T], ACT.Copy)
                fn(osq, mx[:, 3, 0:T], ACT.Square).then_inc(S["osq_ready"], 1)
                act.wait_ge(S["om_done"], n + 1)
                fn(hrt, mx[:, 2, 0:T], ACT.Sqrt, scale=1.0 / P, bias=epst[:, 0:1]).then_inc(S["osd_ready"], 1)
                for s in range(2):
                    read_pair(l, p * 2 + (B_G1 + s), s, tiles_at(gate, p * 4 + 8 + 2 * s, 2), ACT.Sigmoid)\
                        .then_inc(pair_free[s], 1)

            with act.Fori(0, L) as l:
                ffn(l, B_F1, 0)
                act.wait_ge(S["prm_ready"], l + 1)
                norm(l, 2)
                fn(spc[:, 0, :], pcol("lru_lam", 0, 4), ACT.Abs)
                act.drain()
                fn(spc[:, 1, :], spc[:, 0, :], ACT.Exp, scale=-1.0)
                act.drain()
                fn(spc[:, 2, :], spc[:, 1, :], ACT.Ln, bias=1.0).then_inc(S["spln_ready"], 1)
                with act.Fori(0, 3) as i:
                    for s in range(2):
                        read_pair(l, i * 2 + (B_A + s), s, tiles_at(pa, i * 4 + 2 * s, 2), ACT.Copy)\
                            .then_inc(pair_free[s], 1)
                for s in range(2):
                    read_pair(l, B_A + 6 + s, s, pa[:, 12 + s:13 + s, :], ACT.Copy, n=1).then_inc(pair_free[s], 1)
                act.drain().then_inc(S["pa_ready"], 1)
                act.wait_ge(S["lora_in_ready"], l + 1)
                fn(bb[0:CH, :], xs[0:CH, 0, :], ACT.Tanh)
                fn(bb[CH:P, :], xs[CH:P, 0, :], ACT.Copy)
                fn(kp, xs[:, 1, :], ACT.Sigmoid).then_inc(S["lora_act_ready"], 1)
                for s in range(2):
                    read_pair(l, B_B + s, s, pbc[:, 2 * s:2 * s + 2, :], ACT.Copy).then_inc(pair_free[s], 1)
                for kind in range(3):
                    act.wait_ge(S["lora_done"], l * 3 + (kind + 1))
                    for j in range(4):
                        dst, src = lo[:, 4 * kind + j, :], mx[:, j, 0:T]
                        if kind < 2:
                            m = fn(dst, src, ACT.Sigmoid, bias=pcol(("rwkv_w0", "rwkv_a0")[kind], j))
                        else:
                            m = fn(dst, src, ACT.Copy)
                    m.then_inc(S["lora_ready"], 1)
                for s in range(2):
                    read_pair(l, B_B + 2 + s, s, pbc[:, 4 + 2 * s:6 + 2 * s, :], ACT.Copy).then_inc(pair_free[s], 1)
                key_square(l * HP)
                decays(l * HP)
                key_norm(l * HP)
                with act.Fori(0, HP - 1) as p:
                    rwkv_pair(l, p, True)
                rwkv_pair(l, HP - 1, False)
                act.drain().then_inc(S["pbc_ready"], 1)
                act.wait_ge(S["oa_ready"], l * 4 + 5)
                fn(lge, pbc[:, 4:8, :], ACT.Gelu_apprx_tanh)
                for s in range(2):
                    read_pair(l, B_G0 + s, s, gate[:, 2 * s:2 * s + 2, :], ACT.Sigmoid).then_inc(pair_free[s], 1)
                for kind in range(2):
                    act.wait_ge(S["lg_done"], l * 2 + (kind + 1))
                    for j in range(4):
                        m = fn((lr, li)[kind][:, j, :], mx[:, j, 0:T], ACT.Sigmoid,
                               bias=pcol(("lru_ba", "lru_bx")[kind], j))
                    m.then_inc(S["lgate_ready"], 1)
                act.wait_ge(S["lam_ready"], l + 1)
                for j in range(4):
                    fn(la[:, j, :], lr[:, j, :], ACT.Exp, scale=spc[:, 4, j:j + 1])
                for j in range(4):
                    m = fn(lth[:, j, :], lr[:, j, :], ACT.Tanh, scale=spc[:, 5, j:j + 1])
                m.then_inc(S["a_ready"], 1)
                act.wait_ge(S["b2_ready"], l + 1)
                fn(lth, lb_, ACT.Sqrt).then_inc(S["bs_ready"], 1)
                for s in range(2):
                    read_pair(l, B_G0 + 2 + s, s, gate[:, 4 + 2 * s:6 + 2 * s, :], ACT.Sigmoid)\
                        .then_inc(pair_free[s], 1)
                act.wait_ge(S["ob_ready"], l + 1)
                head_functions(l, 0)
                with act.Fori(0, 3) as p:
                    hgrn_head(l, p, True)
                hgrn_head(l, 3, False)
                for j in range(4):
                    read_squared(l, B_OUT + j, j % 2, 2 * j)
                root(l, 3)
                ffn(l, B_F2, 1)

        @block.vector
        def _(dve):
            def tt(out, a, b, op):
                return nc.vector.tensor_tensor(out, a, b, op)

            def mul(out, a, b):
                return nc.vector.tensor_tensor(out, a, b, ALU.mult)

            def stt(out, in0, scalar, in1, op0, op1):
                return nc.vector.scalar_tensor_tensor(out=out, in0=in0, scalar=scalar, in1=in1, op0=op0, op1=op1)

            def ts(out, in0, s1, op0, s2=None, op1=None):
                if op1 is None:
                    return nc.vector.tensor_scalar(out, in0, s1, None, op0)
                return nc.vector.tensor_scalar(out, in0, s1, s2, op0, op1)

            fence = dve.drain

            dve.sem_inc(S["x_new"], 4)
            dve.sem_inc(S["lo_ready"], 2)
            dve.sem_inc(S["h_ready"], 1)
            dve.sem_inc(S["oa_ready"], 1)
            dve.sem_inc(S["oc_ready"], 1)
            dve.sem_inc(pair_free[0], 1)
            dve.sem_inc(pair_free[1], 1)
            nc.vector.memset(epst[:, 0:1], EPS).then_inc(S["eps_ready"], 1)
            nc.vector.memset(epst[:, 1:2], GN_EPS).then_inc(S["eps_ready"], 1)
            nc.vector.memset(E[:, :, :, :], 0.0).then_inc(S["zero_ready"], 1)
            nc.vector.memset(YE[:, :, :], 0.0).then_inc(S["zero_ready"], 1)
            dve.wait_ge(S["const_loaded"], 16)
            dve.wait_ge(S["lg_loaded"], 16)
            dve.wait_ge(S["prm_loaded"], 16)
            tt(lgt[:, 2, :], lg[:, 0, :], lg[:, 1, :], ALU.max)
            fence()
            for i in range(L):
                m = tt(lgt[:, i, :], lg[:, i, :], lgt[:, 2, :], ALU.subtract)
            m.then_inc(S["lgexp_in"], 1)
            dve.wait_ge(S["lgexp_out"], 1)
            tt(lgt[:, 0, :], lgt[:, 2, :], lgt[:, 3, :], ALU.add)
            fence()
            nc.vector.reciprocal(lgt[:, 1, :], lgt[:, 0, :])
            nc.vector.memset(lbt[:, 0, :], 0.0)
            fence()
            mul(lbt[:, 1, :], lgt[:, 3, :], lgt[:, 1, :])
            dve.wait_ge(S["x_loaded"], 16)
            fence()

            def norm_in(l, idx, gname, split=False):
                dve.wait_ge(S["rt_ready"], l * 6 + (idx + 1))
                nc.vector.reciprocal(rs[:, :], rt[:, :])
                fence()

                def low(j):
                    k = slice(2 * j, 2 * j + 2)
                    dve.wait_ge(S["uh_ready"], l * 8 + (idx + j + 1))
                    tt(ul[:, k, :], u[:, k, :], uh[:, k, :].bitcast(F32), ALU.subtract).then_inc(S["u_ready"], 1)

                for j in range(4):
                    for k in (2 * j, 2 * j + 1):
                        m = stt(u[:, k, :], x[:, k, :], pcol(gname, k), rs[:, :], ALU.mult, ALU.mult)
                    m.then_inc(S["uf_ready" if split else "u_ready"], 1)
                    if split and j:
                        low(j - 1)
                if split:
                    low(3)

            def norm_out(l, idx, gname, step):
                dve.wait_ge(S["rt_ready"], l * 6 + (idx + 1))
                nc.vector.reciprocal(rs[:, :], rt[:, :])
                fence()
                for j in range(4):
                    for k in (2 * j, 2 * j + 1):
                        stt(ho[:, k, :], ho[:, k, :], pcol(gname, k), rs[:, :], ALU.mult, ALU.mult)
                    fence()
                    k = slice(2 * j, 2 * j + 2)
                    stt(x[:, k, :], ho[:, k, :], step, x[:, k, :], ALU.mult, ALU.add).then_inc(S["x_new"], 1)

            def ffn(l, b, f):
                names = (("ffn1_pre_g", "ffn1_post_g"), ("ffn2_pre_g", "ffn2_post_g"))[f]
                q = (Q_F1, Q_F2)[f]

                def split_lo(i, j, s):
                    dve.wait_ge(S["hi_ready"], l * NFF + i * 2 + (B_A * f + j + 1))
                    tt(wlo[s][:, :], raw[s][:, :], whi[s][:, :].bitcast(F32), ALU.subtract).then_inc(S["lo_ready"], 1)

                for s in range(2):
                    split_lo(0, s, s)
                norm_in(l, 4 * f, names[0], split=True)
                with dve.Fori(0, KF // 2) as i:
                    split_lo(i, 2, 0)
                    dve.wait_ge(pair_free[0], l * (NPAIR // 2) + i + (q // 2 + 2))
                    wait_block(dve, l, i * 2 + (b + 1))
                    mul(h32, dps[:, 2:4, 0:T], gs[:, :, :]).then_inc(pair_free[1], 1)
                    fence()
                    nc.vector.tensor_copy(tiles_at(hfh, i * 2, 2), h32)
                    fence()
                    tt(tiles_at(hfl, i * 2, 2), h32, tiles_at(hfh, i * 2, 2).bitcast(F32), ALU.subtract)
                    dve.drain().then_inc(S["h_ready"], 1)
                    split_lo(i, 3, 1)
                for j in range(2, 12):
                    split_lo(0, KF + j, j % 2)
                norm_out(l, 4 * f + 1, names[1], 0.5)

            def token_shift(l, src, k0, nk, strided, parts=(0, 1)):
                mu0 = PCOL["rwkv_mu"]
                if strided is None:
                    s, sh, mu = src[:, k0:k0 + nk, :], shift_in[:, k0:k0 + nk, :], prm[:, mu0 + k0:mu0 + k0 + nk]
                else:
                    s = src[:, 0:12, :].rearrange("p (i j) t -> p i j t", i=3)[:, :, bass.ds(strided, 1), :]\
                        .rearrange("p i j t -> p i (j t)")
                    sh = shift_in[:, 0:12, :].rearrange("p (i j) t -> p i j t", i=3)[:, :, bass.ds(strided, 1), :]\
                        .rearrange("p i j t -> p i (j t)")
                    mu = prm[:, mu0:mu0 + 12].rearrange("p (i j) -> p i j", i=3)[:, :, bass.ds(strided, 1)]\
                        .rearrange("p i j -> p (i j)")
                d = dd[:, 0:nk, :]
                ds_, sd_ = (v[:, :, TP:T].rearrange("p i (b t) -> p i b t", b=NB) for v in (d, s))
                if 0 in parts:
                    tt(d[:, :, 1:TP], s[:, :, 0:TP - 1], s[:, :, 1:TP], ALU.subtract)
                    ts(d[:, :, 0:1], s[:, :, 0:1], -1.0, ALU.mult)
                    for i in range(nk):
                        tt(ds_[:, i, :, 1:TS], sd_[:, i, :, 0:TS - 1], sd_[:, i, :, 1:TS], ALU.subtract)
                        tt(ds_[:, i, :, 0], sh[:, i, :], sd_[:, i, :, 0], ALU.subtract)
                    fence()
                if 1 not in parts:
                    return None
                mul(d, d, mu.unsqueeze(2).to_broadcast([P, nk, T]))
                fence()
                return tt(xs[:, 0:nk, :], d, s, ALU.add)

            def half(kind, h, a, b):
                r = slice(CH * h, CH * h + CH)
                return mul(E[r, kind, :, r], chunks(a[r, :]), chunks(b[r, :]))

            r_, k_, v_ = (xs[:, i, :] for i in range(3))

            def prepare(l, p, step):
                n = l * HP + p
                a_ = tile_at(lo, p + 4)
                if step == 0:
                    token_shift(l, pa, 0, 3, p, parts=(0,))
                elif step == 1:
                    token_shift(l, pa, 0, 3, p, parts=(1,))
                    fence()
                    mul(kk0, k_, pcol("rwkv_k_k", p).to_broadcast([P, T])).then_inc(S["kk0_ready"], 1)
                elif step == 2:
                    ts(logd, tile_at(lo, p), -EM05, ALU.mult)
                    ts(bb, a_, 1.0, ALU.subtract, pcol("rwkv_k_a", p), ALU.mult)
                    fence()
                    nc.vector.tensor_tensor_scan(cum, seg_a, logd, 0.0, ALU.mult, ALU.add)
                    stt(kp, bb, 1.0, k_, ALU.add, ALU.mult)
                    fence()
                elif step == 3:
                    tt(cumm, cum, logd, ALU.subtract).then_inc(S["cumm_ready"], 1)
                    stt(rkr, r_, pcol("rwkv_r_k", p), kp, ALU.mult, ALU.mult).then_inc(S["rkr_ready"], 1)
                elif step == 4:
                    dve.wait_ge(S["rk_done"], n + 1)
                    mul(tile_at(oa, p), mx[:, 1, 0:T], v_)
                else:
                    dve.wait_ge(S["norm_ready"], n + 1)
                    ts(nrm, nrm, 1e-12, ALU.max)
                    fence()
                    nc.vector.reciprocal(nrm, nrm)
                    fence()
                    mul(kksq, kk0, nrm)
                    fence()
                    mul(bb, kksq, a_)
                    fence()

            def masks(l, p, chunks_):
                n = l * HP + p
                for c in chunks_:
                    dve.wait_ge(S["abq_done"], n * 5 + (c + 1))
                    mask = mask_p if c < NCH - 1 else mask_s
                    mul(abq[:, c, :, :].rearrange("p (a k) s -> p a (k s)", a=2),
                        mx[:, c % 2, :].rearrange("p (a m) -> p a m", a=2),
                        mask.unsqueeze(1).to_broadcast([P, 2, 2 * P])).then_inc(S["abq_ready"], 1)

            def rwkv_pair(l, p, more):
                n = l * HP + p
                nc.vector.tensor_copy(gchunk[:, :], chunks(gam)[:, 0:NCH - 1, CH - 1])
                nc.vector.tensor_copy(gstream[:, :], gam[:, TP:T].rearrange("p (b t) -> p b t", b=NB)[:, :, TS - 1])
                fence()

                def level_part(li):
                    nch = NCH if li <= 2 else NCH - 1
                    return mul(ao[li % 2][:, 0:nch, :], abq[:, 0:nch, 0, :],
                               level[:, li, :].unsqueeze(1).to_broadcast([P, nch, P]))

                level_part(0).then_inc(S["ao_ready"], 1)
                fence()
                identb = ident.unsqueeze(1).to_broadcast([P, NCH, P])
                tt(tinvt, identb, ao[0], ALU.subtract)
                level_part(1).then_inc(S["ao_ready"], 1)
                if more:
                    prepare(l, p + 1, 0)
                dve.wait_ge(S["z_done"], n * 6 + 1)
                tt(tinv, identb, chunks(mx01[:, 0:640]), ALU.subtract).then_inc(S["t_ready"], 1)
                for li in range(1, 6):
                    nch = NCH if li <= 2 else NCH - 1
                    nt = NCH if li < 2 else NCH - 1 if li < 5 else 0
                    fence()
                    if li < 5:
                        level_part(li + 1).then_inc(S["ao_ready"], 1)
                    if more:
                        if li == 1:
                            dve.wait_ge(S["ve_ready"], n + 1)
                        prepare(l, p + 1, li)
                    dve.wait_ge(S["pt_done"], n * 5 + li)
                    if nt:
                        tt(tinv[:, 0:nt, :], tinv[:, 0:nt, :],
                           mx23[:, 0:nt * P].rearrange("p (c s) -> p c s", c=nt), ALU.subtract)
                    tt(tinvt[:, 0:nch, :], tinvt[:, 0:nch, :],
                       mx01[:, 0:nch * P].rearrange("p (c s) -> p c s", c=nch), ALU.subtract)\
                        .then_inc(S["t_ready"], 1)
                dve.wait_ge(S["ss_free"], n + 1)
                for c in range(NCH - 1):
                    g = gchunk[:, c:c + 1]
                    dve.wait_ge(S["p_done"], n * 4 + (c + 1))
                    ts(pn[:, :], mx[:, 0, 0:CH], -1.0, ALU.mult).then_inc(S["pn_ready"], 1)
                    if c:
                        ts(stg[:, :], st[:, c, :], g, ALU.mult)
                    dve.wait_ge(S["u_done"], n * 4 + (c + 1))
                    nc.vector.tensor_copy(uu[:, :], mx[:, 1, 0:CH]).then_inc(S["uc_ready"], 1)
                    fence()
                    dve.wait_ge(S["s_done"], n * 4 + (c + 1))
                    if c:
                        stt(st[:, c + 1, :], mx[:, 3, 0:CH], g, stg[:, :], ALU.mult, ALU.add)\
                            .then_inc(S["s_ready"], 1)
                    else:
                        ts(st[:, 1, :], mx[:, 3, 0:CH], g, ALU.mult).then_inc(S["s_ready"], 1)
                    fence()
                    if more:
                        if c == 0:
                            dve.wait_ge(S["gam_ready"], n + 2)
                        half(2 + c // 2, c % 2, bb if c < 2 else kp, igam)
                dve.wait_ge(S["y_done"], n + 1)
                for h in range(2):
                    r = slice(CH * h, CH * h + CH)
                    m = nc.vector.tensor_copy(YE[r, 0:NCH - 1, r], mx[r, 2, 0:TP].rearrange("p (c v) -> p c v", v=CH))
                m.then_inc(S["ye_ready"], 1)

                maskb = mask_b.unsqueeze(2).to_broadcast([P, NB, CH])

                def own_stream(src):
                    mul(tmpb, streams(src), maskb)
                    fence()
                    nc.vector.tensor_reduce(ps1[:, :], tmpb.rearrange("p b v -> p v b"), AX.X, ALU.add)
                    fence()

                dve.wait_ge(S["sp_done"], n + 1)
                own_stream(mx[:, 0, :])
                stt(pn[:, :], mx[:, 1, 0:CH], -1.0, ps1[:, :], ALU.mult, ALU.subtract).then_inc(S["spn_ready"], 1)
                if more:
                    for h in range(2):
                        half(0, h, kksq, gamm)
                dve.wait_ge(S["su_done"], n + 1)
                nc.vector.tensor_copy(uu[:, :], mx[:, 0, 0:CH])
                fence()
                mul(ub, uu[:, :].unsqueeze(1).to_broadcast([P, NB, CH]), maskb)
                mul(vb, vtok[:, NCH - 1, :].unsqueeze(1).to_broadcast([P, NB, CH]), maskb)\
                    .then_inc(S["suc_ready"], 1)
                dve.wait_ge(S["sy_done"], n + 1)
                own_stream(mx[:, 2, :])
                for h in range(2):
                    r = slice(CH * h, CH * h + CH)
                    m = tt(YE[r, NCH - 1, r], mx[r, 3, 0:CH], ps1[r, :], ALU.add)
                m.then_inc(S["ye4_ready"], 1)
                dve.wait_ge(S["sst_done"], n + 1)
                tt(ssn[:, :, :], ss[:, :, :], streams(mx[:, 0, :]), ALU.add)
                fence()
                mul(ssn[:, :, :], ssn[:, :, :], gstream[:, :].unsqueeze(2).to_broadcast([P, NB, CH]))\
                    .then_inc(S["ssn_ready"], 1)
                if more:
                    for h in range(2):
                        m = half(1, h, r_, gam)
                    m.then_inc(S["e_ready"], 1)
                dve.wait_ge(S["mean_done"], n + 1)
                stt(dev, mx[:, 2, 0:T], -1.0 / CH, y_, ALU.mult, ALU.add).then_inc(S["dev_ready"], 1)
                if more:
                    masks(l, p + 1, (0, 1))
                dve.wait_ge(S["sd_ready"], n + 1)
                nc.vector.reciprocal(rsd, sd)
                fence()
                mul(dev, dev, rsd)
                fence()
                ts(dev, dev, pcol("rwkv_ln_g", p), ALU.mult, pcol("rwkv_ln_b", p), ALU.add)
                if more:
                    masks(l, p + 1, (2,))
                fence()
                tt(dev, dev, tile_at(oa, p), ALU.add)
                fence()
                mul(tile_at(oa, p), dev, tile_at(lo, p + 8)).then_inc(S["oa_ready"], 1)
                if more:
                    masks(l, p + 1, (3, 4))
                fence()

            def rglru(l):
                dve.wait_ge(S["pbc_ready"], l + 1)
                dve.wait_ge(S["lru_loaded"], l * 32 + 32)
                xps = xp[:, :, 3 + TP:XPW].rearrange("p k (b n) -> p k b n", b=NB)
                xcs = xc[:, :, TP:T].rearrange("p k (b n) -> p k b n", b=NB)
                nc.vector.memset(xp[:, :, 0:3], 0.0)
                nc.vector.tensor_copy(xp[:, :, 3:3 + TP], pbc[:, 0:4, 0:TP])
                for k in range(4):
                    nc.vector.tensor_copy(xps[:, k, :, 0:3], conv_in[:, k, :, :])
                    nc.vector.tensor_copy(xps[:, k, :, 3:3 + TS],
                                          pbc[:, k, TP:T].rearrange("p (b n) -> p b n", b=NB))
                fence()
                for j in range(4):
                    for k in range(4):
                        w = pcol("lru_conv_w", 4 * j + k)
                        for dst, src in ((xc[:, k, 0:TP], xp[:, k, j:j + TP]), (xcs[:, k, :, :], xps[:, k, :, j:j + TS])):
                            if j == 0:
                                m = ts(dst, src, w, ALU.mult, pcol("lru_conv_b", k), ALU.add)
                            else:
                                m = stt(dst, src, w, dst, ALU.mult, ALU.add)
                    if j < 3:
                        fence()
                m.then_inc(S["xc_ready"], 1)
                dve.wait_ge(S["lru_free"], l + 1)
                nc.vector.tensor_copy(conv_out[:, :, 0, :], xp[:, :, TP:TP + 3])
                for k in range(4):
                    nc.vector.tensor_copy(conv_out[:, k, 1:NB + 1, :], xps[:, k, :, TS:TS + 3])
                dve.wait_ge(S["lgate_ready"], l * 2 + 2)
                mul(li, li, xc)
                dve.wait_ge(S["a_ready"], l + 1)
                mul(lb_, la, la)
                fence()
                stt(lb_, lb_, 1.0, lth, ALU.add, ALU.mult).then_inc(S["b2_ready"], 1)
                las, lbs = (v[:, :, TP:T].rearrange("p k (b n) -> p k b n", b=NB)[:, :, :, 0] for v in (la, lb_))
                h0 = lru_out[:, :, 1:NB + 1]
                mul(h0, las, lru_in[:, :, :])
                fence()
                mul(la, la, seg_b.unsqueeze(1).to_broadcast([P, 4, T]))
                dve.wait_ge(S["bs_ready"], l + 1)
                mul(lb_, lth, li)
                fence()
                tt(lbs, lbs, h0, ALU.add)
                fence()
                for k in range(4):
                    nc.vector.tensor_tensor_scan(lr[:, k, :], la[:, k, :], lb_[:, k, :], 0.0, ALU.mult, ALU.add)
                fence()
                nc.vector.tensor_copy(lru_out[:, :, 0:1], lr[:, :, TP - 1:TP])
                nc.vector.tensor_copy(lru_out[:, :, 1:NB + 1],
                                      lr[:, :, TP:T].rearrange("p k (b n) -> p k b n", b=NB)[:, :, :, TS - 1])\
                    .then_inc(S["lru_out_ready"], 1)
                mul(ob, lr, lge).then_inc(S["ob_ready"], 1)
                nc.vector.tensor_copy(lbc[:, 1, :], tile_at(lbt, l))
                fence()
                ts(lbc[:, 0, :], lbc[:, 1, :], -1.0, ALU.mult, 1.0, ALU.add)
                fence()

            def hgrn_head(l, p):
                n = l * 4 + p
                dve.wait_ge(S["hsig_ready"], n + 1)
                mul(hq, sgq, tile_at(pbc, p + 8))
                ts(hf, sgf, lbc[:, 0, :][:, bass.ds(p, 1)], ALU.mult, lbc[:, 1, :][:, bass.ds(p, 1)], ALU.add)
                mul(gzs, sgz, tile_at(pbc, p + 20))
                nc.vector.memset(suf, 1.0)
                nc.vector.memset(att, 0.0)
                fence()
                nc.vector.tensor_copy(pre, hf)
                ts(hk, hf, -1.0, ALU.mult, 1.0, ALU.add).then_inc(S["hq_ready"], 1)

                def keep(mask, bank, small=True):
                    mask = mask.bitcast(U32)
                    nc.vector.copy_predicated(att[:, 0:TP].rearrange("p (c t) -> p c t", c=2),
                                              mask.unsqueeze(1).to_broadcast([P, 2, P]),
                                              mx[:, bank, 0:TP].rearrange("p (c t) -> p c t", c=2))
                    if small:
                        nc.vector.copy_predicated(att[0:CH, TP:T], mask[0:CH, 0:CH], mx[0:CH, bank, TP:T])

                def factors(li):
                    h = 1 << li
                    e = T if li < 3 else TP

                    def part(v, which):
                        return v[:, 0:e].rearrange("p (n w) -> p n w", w=2 * h)[:, :, which * h:which * h + h]

                    def edge(v, which):
                        last = v[:, 0:e].rearrange("p (n w) -> p n w", w=2 * h)[:, :, which * h + h - 1:which * h + h]
                        return last.to_broadcast([P, e // (2 * h), h])

                    fence()
                    mul(part(qps[li % 2], 1), part(hq, 1), part(pre, 1))
                    mul(part(kss[li % 2], 0), part(hk, 0), part(suf, 0)).then_inc(S["qk_ready"], 1)
                    mul(part(suf, 0), part(suf, 0), edge(pre, 1))
                    fence()
                    mul(part(pre, 1), part(pre, 1), edge(pre, 0))

                factors(0)
                wait_apart(dve, "att_done", n * 8 + 1)
                keep(ident, 0)
                for li in range(7):
                    if li < 6:
                        factors(li + 1)
                    else:
                        fence()
                        mul(kss[1], hk, suf).then_inc(S["hkt_ready"], 1)
                        mul(qps[1], hq, pre)
                    wait_apart(dve, "att_done", n * 8 + (li + 2))
                    keep(level[:, li, :], (li + 1) % 2, li < 3)
                fence()
                dve.wait_ge(S["hs_free"], n + 1)
                dve.wait_ge(S["ht_ready"], n * 2 + 1)
                mul(hvb[0:CH, :, :], vt3[0:CH, 2, :].unsqueeze(1).to_broadcast([CH, NB, P]),
                    mask_b[0:CH, :].unsqueeze(2).to_broadcast([CH, NB, P])).then_inc(S["hb_ready"], 1)
                glast = pre[:, TP:T].rearrange("p (b t) -> p b t", b=NB)[:, :, TS - 1:TS]
                dve.wait_ge(S["hs_loaded"], n * 16 + 16)
                mul(hsn[:, :, :], hs[:, :, :], glast.to_broadcast([P, NB, P]))
                dve.wait_ge(S["hst1_done"], n + 1)
                nc.vector.tensor_copy(hst[:, 0, :], mx[:, 2, 0:P])
                fence()
                stt(hst[:, 1, :], hst[:, 0, :], pre[:, TP - 1:TP], mx[:, 2, P:2 * P], ALU.mult, ALU.add)\
                    .then_inc(S["hst1_ready"], 1)
                dve.wait_ge(S["hst_done"], n + 1)
                tt(hsn[:, :, :], hsn[:, :, :], streams(mx01), ALU.add).then_inc(S["hsn_ready"], 1)
                dve.wait_ge(S["osd_ready"], n + 1)
                nc.vector.reciprocal(hrs, hrt)
                fence()
                mul(osb, osb, hrs)
                fence()
                stt(tile_at(oc, p), osb, pcol("hgrn_norm_g", p), gzs, ALU.mult, ALU.mult).then_inc(S["oc_ready"], 1)
                fence()

            with dve.Fori(0, L) as l:
                nc.vector.tensor_copy(prm[:, :], tile_at(prm_all, l)).then_inc(S["prm_ready"], 1)
                ffn(l, B_F1, 0)
                norm_in(l, 2, "mix_pre_g")
                ts(spc[:, 3, :], pcol("lru_lam", 0, 4), -1.0, ALU.mult, 0.0, ALU.max)
                fence()
                dve.wait_ge(S["spln_ready"], l + 1)
                tt(spc[:, 3, :], spc[:, 3, :], spc[:, 2, :], ALU.add)
                fence()
                ts(spc[:, 4, :], spc[:, 3, :], -8.0, ALU.mult)
                ts(spc[:, 5, :], spc[:, 3, :], 8.0, ALU.mult).then_inc(S["lam_ready"], 1)
                dve.wait_ge(S["pa_ready"], l + 1)
                dve.wait_ge(S["shift_loaded"], l * 16 + 16)
                token_shift(l, pa, 12, 2, None).then_inc(S["lora_in_ready"], 1)
                dve.wait_ge(S["shift_free"], l + 1)
                nc.vector.tensor_copy(shift_out[:, :, 0:1], pa[:, :, TP - 1:TP])
                nc.vector.tensor_copy(shift_out[:, :, 1:NB + 1],
                                      pa[:, :, TP:T].rearrange("p k (b n) -> p k b n", b=NB)[:, :, :, TS - 1])\
                    .then_inc(S["shift_out_ready"], 1)
                fence()
                prepare(l, 0, 0)
                dve.wait_ge(S["lora_act_ready"], l + 1)
                prepare(l, 0, 1)
                dve.wait_ge(S["lora_ready"], l * 3 + 3)
                for step in range(2, 6):
                    prepare(l, 0, step)
                dve.wait_ge(S["gam_ready"], l * HP + 1)
                for kind, a, b in ((0, kksq, gamm), (1, r_, gam), (2, bb, igam), (3, kp, igam)):
                    for h in range(2):
                        m = half(kind, h, a, b)
                m.then_inc(S["e_ready"], 1)
                masks(l, 0, range(NCH))
                with dve.Fori(0, HP - 1) as p:
                    rwkv_pair(l, p, True)
                rwkv_pair(l, HP - 1, False)
                rglru(l)
                with dve.Fori(0, 4) as p:
                    hgrn_head(l, p)
                dve.wait_ge(S["hs_free"], l * 4 + 5)
                for br in range(3):
                    for s in range(2):
                        for half in range(2):
                            if half:
                                wait_block(dve, l, B_PROJ + 2 * br + s)
                            else:
                                dve.wait_ge(S["proj_half"], l * 6 + (2 * br + s + 1))
                            k = 4 * s + 2 * half
                            dst = merged[:, k:k + 2, :] if br == 0 else xs[:, 0:2, :]
                            mul(dst, dps[:, 2 * half:2 * half + 2, 0:T], gate[:, 8 * br + k:8 * br + k + 2, :])\
                                .then_inc(pair_free[half], 1)
                            if br:
                                fence()
                                m = tt(merged[:, k:k + 2, :], merged[:, k:k + 2, :], xs[:, 0:2, :], ALU.add)
                                fence()
                m.then_inc(S["merged_ready"], 1)
                norm_out(l, 3, "mix_post_g", 1.0)
                ffn(l, B_F2, 1)


def tiles_first(a, n):
    a = a.reshape(a.shape[0], n, P, *a.shape[2:])
    return np.moveaxis(a, 2, 1)


def weight_blocks(w, k_parts, width, l):
    w = w[l].reshape(w.shape[1] // P, P, w.shape[2])
    out = []
    for c in range(0, w.shape[2], width):
        k = 0
        for kt in k_parts:
            part = np.moveaxis(w[k:k + kt, :, c:c + width], 0, 1).reshape(P, -1)
            blk = np.zeros((P, BLK), np.float32)
            blk[:, :part.shape[1]] = part
            out.append(blk)
            k += kt
    return out


def kernel(**inputs):
    import concourse.bacc as _bacc
    from concourse.bass_utils import run_bass_kernel_spmd as _run

    I = {k: np.asarray(v) for k, v in inputs.items()}
    blocks = []
    for l in range(L):
        for f in ("ffn1", "ffn2"):
            g, u_ = (weight_blocks(I[f"{f}_w{c}"], [KD], 256, l) for c in "gu")
            ff = [b for two in zip(g, u_) for b in two] + weight_blocks(I[f"{f}_wd"], [8, 8, 6], 256, l)
            if f == "ffn1":
                blocks += ff
                w = I["w_in"]
                blocks += weight_blocks(w[:, :, 0:1536], [KD], 256, l)
                blocks += weight_blocks(w[:, :, 1536:1792], [KD], P, l)
                blocks += weight_blocks(w[:, :, 1792:], [KD], 256, l)
                for name in "abc":
                    blocks += weight_blocks(I[f"proj_{name}"], [4], 512, l)
                blocks += weight_blocks(I["w_out"], [KD], 256, l)
            else:
                blocks += ff
    arrays = {"wstream": np.stack(blocks)}
    small = np.zeros((L, P, 4, 512), np.float32)
    small[:, 0:64, 0], small[:, 64:128, 0], small[:, :, 1] = I["rwkv_w2"], I["rwkv_a2"], I["rwkv_g2"]
    for i, name in enumerate(("lru_wa", "lru_wx")):
        for g in range(8):
            r = 64 * (g % 2)
            small[:, r:r + 64, 2 + i, 64 * g:64 * g + 64] = I[name][:, g]
    arrays["smallw"] = small
    arrays["params"] = np.concatenate([tiles_first(I[n].reshape(L, w * P), w) for n, w in PARAMS], 2)
    arrays["logits"] = np.moveaxis(I["hgrn_lb_logits"].reshape(L, 4, P), 2, 0)
    arrays["consts"] = constants()[0]
    rows = np.concatenate([I["x_prompt"].reshape(TP, D), I["x_sample"].reshape(T - TP, D)], 0)
    arrays["xT"] = np.moveaxis(rows.T.reshape(KD, P, T), 1, 0)
    arrays["st_shift"] = tiles_first(np.moveaxis(I["state_shift"], 1, 2), 14)
    arrays["st_lru"] = tiles_first(np.moveaxis(I["state_lru"], 1, 2), 4)
    conv = np.moveaxis(I["state_conv"], 3, 1)
    arrays["st_conv"] = tiles_first(conv, 4).reshape(L, P, 4, NB * 3)
    rw = I["state_rwkv"].reshape(L, NB, HP, 2, 64, 64)
    arrays["st_rwkv"] = rw.transpose(0, 2, 3, 5, 1, 4).reshape(L * HP, P, NB, 64)
    arrays["st_hgrn"] = I["state_hgrn"].transpose(0, 2, 3, 1, 4).reshape(L * 4, P, NB, P)
    outs = {"yT": (P, KD, T), "o_shift": (L, P, 14, NB + 1), "o_rwkv": (L * HP, P, NB + 1, 64),
            "o_lru": (L, P, 4, NB + 1), "o_conv": (L, P, 4, (NB + 1) * 3), "o_hgrn": (L * 4, P, NB + 1, P)}

    nc = _bacc.Bacc("TRN2", target_bir_lowering=False, num_devices=1)
    arrays = {k: np.ascontiguousarray(v) for k, v in arrays.items()}
    args = {k: nc.dram_tensor(f"in_{k}", v.shape, F32, kind="ExternalInput").ap() for k, v in arrays.items()}
    args.update({k: nc.dram_tensor(f"out_{k}", s, F32, kind="ExternalOutput").ap() for k, s in outs.items()})
    trunk(nc, **args)
    r = _run(nc, [{f"in_{k}": v for k, v in arrays.items()}], core_ids=[0]).results[0]

    y = np.moveaxis(r["out_yT"], 0, 1).reshape(D, T).T
    shift = np.moveaxis(r["out_o_shift"], 1, 2).reshape(L, 1792, NB + 1).transpose(0, 2, 1)
    rwkv = r["out_o_rwkv"].reshape(L, HP, 2, 64, NB + 1, 64).transpose(0, 4, 1, 2, 5, 3)
    rwkv = rwkv.reshape(L, NB + 1, 8, 64, 64)
    lru = np.moveaxis(r["out_o_lru"], 1, 2).reshape(L, 512, NB + 1).transpose(0, 2, 1)
    conv = np.moveaxis(r["out_o_conv"].reshape(L, P, 4, NB + 1, 3), 1, 2).reshape(L, 512, NB + 1, 3)
    conv = conv.transpose(0, 2, 3, 1)
    hgrn = r["out_o_hgrn"].reshape(L, 4, P, NB + 1, P).transpose(0, 3, 1, 2, 4)
    c = np.ascontiguousarray
    return (c(y[:TP].reshape(1, TP, D)), c(y[TP:].reshape(NB, TS, D)),
            *(c(a[:, :1]) for a in (rwkv, shift, lru, conv, hgrn)),
            *(c(a[:, 1:]) for a in (rwkv, shift, lru, conv, hgrn)))
```
